# Optimizing a Trainium2 kernel written in Bass

```python
import jax, jax.numpy as jnp
from jax import lax
import numpy as np

D_MODEL = 1024
BATCH = 1
SEQ = 256
DEPTH = 2

LRU_WIDTH = 512
LRU_BLOCKS = 8
LRU_BLOCK = LRU_WIDTH // LRU_BLOCKS
LRU_C = 8.0
CONV_WIDTH = 4
RWKV_HEADS = 8
RWKV_HEAD = 64
RWKV_WIDTH = RWKV_HEADS * RWKV_HEAD
W_LORA = 64
A_LORA = 64
G_LORA = 128
LN_X_EPS = 1e-5 * RWKV_HEAD
MLSTM_HEADS = 8
MLSTM_HEAD = 128
MLSTM_WIDTH = MLSTM_HEADS * MLSTM_HEAD
MLSTM_CHUNK = 128
D_FF = 2816
N_EXPERTS = 8
TOP_K = 2
EXPERT_BLOCK = 256
RMS_EPS = 1e-6
EVEN_IN = 2 * LRU_WIDTH + 3 * RWKV_WIDTH + W_LORA + A_LORA + G_LORA
ODD_IN = 2 * MLSTM_WIDTH + 2 * MLSTM_HEADS

kernel_name = 'hybrid_rglru_rwkv7_mlstm_moe'

def rms_norm(x, w):
    x32 = x.astype(jnp.float32)
    y = x32 * lax.rsqrt(jnp.mean(x32 * x32, axis=-1, keepdims=True) + RMS_EPS)
    return y.astype(x.dtype) * w

def causal_dwconv(x, w, b):
    y = lax.conv_general_dilated(
        x, w[:, None, :].astype(x.dtype), window_strides=(1,),
        padding=[(w.shape[0] - 1, 0)],
        dimension_numbers=('NWC', 'WIO', 'NWC'),
        feature_group_count=x.shape[-1])
    return y + b

def token_shift(x):
    return jnp.pad(x, ((0, 0), (1, 0), (0, 0)))[:, :-1]

def swiglu(x, w1, w3, w2):
    return (jax.nn.silu(x @ w1) * (x @ w3)) @ w2

def linear_recurrence(a, b):
    def combine(l, r):
        return l[0] * r[0], r[0] * l[1] + r[1]
    return lax.associative_scan(combine, (a, b), axis=1)[1]

def rg_lru(xc, gate_a_w, gate_a_b, gate_x_w, gate_x_b, lam):
    B, S, _ = xc.shape
    xb = xc.reshape(B, S, LRU_BLOCKS, LRU_BLOCK)
    r = jax.nn.sigmoid(jnp.einsum('bsgi,gij->bsgj', xb, gate_a_w).reshape(B, S, LRU_WIDTH) + gate_a_b)
    i = jax.nn.sigmoid(jnp.einsum('bsgi,gij->bsgj', xb, gate_x_w).reshape(B, S, LRU_WIDTH) + gate_x_b)
    log_a = -LRU_C * r * jax.nn.softplus(-lam)
    is_first = (jnp.arange(S) == 0)[None, :, None]
    mult = jnp.where(is_first, 1.0, jnp.sqrt(-jnp.expm1(2.0 * log_a)))
    return linear_recurrence(jnp.exp(log_a), mult * i * xc)

def rwkv7_scan(r, w, k, v, kk, a):
    B, S, H, N = r.shape

    def step(state, inp):
        r_t, w_t, k_t, v_t, kk_t, a_t = inp
        sa = jnp.einsum('bhvk,bhk->bhv', state, -kk_t)
        state = (state * w_t[:, :, None, :]
                 + sa[..., None] * (kk_t * a_t)[:, :, None, :]
                 + v_t[..., None] * k_t[:, :, None, :])
        return state, jnp.einsum('bhvk,bhk->bhv', state, r_t)

    xs = tuple(jnp.moveaxis(t, 1, 0) for t in (r, w, k, v, kk, a))
    _, y = lax.scan(step, jnp.zeros((B, H, N, N), jnp.float32), xs)
    return jnp.moveaxis(y, 0, 1)

def rwkv7_mix(p_rw, shift_mu, w0, w_up, a0, a_up, g_up, k_k, k_a, r_k, ln_x_w, ln_x_b):
    B, S, _ = p_rw.shape
    p = p_rw.astype(jnp.float32)
    p = p + shift_mu * (token_shift(p) - p)
    cuts = [RWKV_WIDTH, 2 * RWKV_WIDTH, 3 * RWKV_WIDTH, 3 * RWKV_WIDTH + W_LORA,
            3 * RWKV_WIDTH + W_LORA + A_LORA]
    r, k, v, xw, xa, xg = jnp.split(p, cuts, axis=-1)
    w_log = -jax.nn.softplus(-(w0 + jnp.tanh(xw) @ w_up)) - 0.5
    decay = jnp.exp(-jnp.exp(w_log))
    a = jax.nn.sigmoid(a0 + xa @ a_up)
    g = jax.nn.sigmoid(xg) @ g_up

    def heads(t):
        return t.reshape(B, S, RWKV_HEADS, RWKV_HEAD)

    kk = heads(k * k_k)
    kk = kk / jnp.maximum(jnp.sqrt(jnp.sum(kk * kk, axis=-1, keepdims=True)), 1e-12)
    r, k, v, decay, a = heads(r), heads(k), heads(v), heads(decay), heads(a)
    k = k * (1.0 + (a - 1.0) * k_a.reshape(RWKV_HEADS, RWKV_HEAD))
    y = rwkv7_scan(r, decay, k, v, kk, a)
    mu = jnp.mean(y, axis=-1, keepdims=True)
    var = jnp.mean(jnp.square(y - mu), axis=-1, keepdims=True)
    y = ((y - mu) * lax.rsqrt(var + LN_X_EPS)).reshape(B, S, RWKV_WIDTH) * ln_x_w + ln_x_b
    bonus = jnp.sum(r * k * r_k, axis=-1, keepdims=True) * v
    y = y + bonus.reshape(B, S, RWKV_WIDTH)
    return y * g

def mlstm_chunkwise(q, k, v, ig, logf):
    B, H, S, dk = q.shape
    dv = v.shape[-1]
    L = MLSTM_CHUNK
    nc = S // L
    q = q * (dk ** -0.5)

    def chunks(t):
        return jnp.moveaxis(t.reshape(t.shape[:2] + (nc, L) + t.shape[3:]), 2, 0)

    causal = jnp.tril(jnp.ones((L, L), dtype=bool))

    def step(carry, inp):
        C, n, m = carry
        qc, kc, vc, igc, lfc = inp
        b = jnp.cumsum(lfc, axis=-1)
        dlog = jnp.where(causal, b[..., :, None] - b[..., None, :] + igc[..., None, :], -jnp.inf)
        inter = b + m[..., None]
        m_t = jnp.maximum(inter, jnp.max(dlog, axis=-1))
        dmat = jnp.exp(dlog - m_t[..., None])
        s = jnp.einsum('bhtd,bhsd->bhts', qc, kc) * dmat
        sc = jnp.exp(inter - m_t)
        num = sc[..., None] * jnp.einsum('bhtd,bhde->bhte', qc, C) + jnp.einsum('bhts,bhse->bhte', s, vc)
        den = sc * jnp.einsum('bhtd,bhd->bht', qc, n) + jnp.sum(s, axis=-1)
        h = num / jnp.maximum(jnp.abs(den), jnp.exp(-m_t))[..., None]
        b_last = b[..., -1]
        wlog = b_last[..., None] - b + igc
        m_new = jnp.maximum(b_last + m, jnp.max(wlog, axis=-1))
        wts = jnp.exp(wlog - m_new[..., None])
        dec = jnp.exp(b_last + m - m_new)
        C = dec[..., None, None] * C + jnp.einsum('bhs,bhsd,bhse->bhde', wts, kc, vc)
        n = dec[..., None] * n + jnp.einsum('bhs,bhsd->bhd', wts, kc)
        return (C, n, m_new), h

    init = (jnp.zeros((B, H, dk, dv), jnp.float32), jnp.zeros((B, H, dk), jnp.float32),
            jnp.zeros((B, H), jnp.float32))
    _, h = lax.scan(step, init, (chunks(q), chunks(k), chunks(v), chunks(ig), chunks(logf)))
    return jnp.moveaxis(h, 0, 2).reshape(B, H, S, dv)

def moe_swiglu(xn, w_router, w1, w3, w2):
    B, S, D = xn.shape
    T = B * S
    M = T * TOP_K
    xt = xn.reshape(T, D)
    logits = (xt @ w_router).astype(jnp.float32)
    top_logit, top_idx = lax.top_k(logits, TOP_K)
    gates = jax.nn.softmax(top_logit, axis=-1)
    flat_e = top_idx.reshape(-1)
    flat_tok = jnp.repeat(jnp.arange(T, dtype=jnp.int32), TOP_K)
    order = jnp.argsort(flat_e)
    sorted_e = flat_e[order]
    sorted_tok = flat_tok[order]
    sorted_g = gates.reshape(-1)[order]
    counts = jnp.bincount(flat_e, length=N_EXPERTS)
    padded = ((counts + EXPERT_BLOCK - 1) // EXPERT_BLOCK) * EXPERT_BLOCK
    start = jnp.cumsum(counts) - counts
    pend = jnp.cumsum(padded)
    pstart = pend - padded
    dest = pstart[sorted_e] + (jnp.arange(M) - start[sorted_e])
    P = ((M + EXPERT_BLOCK - 1) // EXPERT_BLOCK + N_EXPERTS) * EXPERT_BLOCK
    nblk = P // EXPERT_BLOCK
    buf = jnp.zeros((P, D), xn.dtype).at[dest].set(xt[sorted_tok])
    blk_e = jnp.clip(jnp.searchsorted(pend, jnp.arange(nblk) * EXPERT_BLOCK, side='right'),
                     0, N_EXPERTS - 1)

    def expert_block(args):
        xb, e = args
        return swiglu(xb, w1[e], w3[e], w2[e])

    yb = lax.map(expert_block, (buf.reshape(nblk, EXPERT_BLOCK, D), blk_e))
    y_slot = yb.reshape(P, D)[dest] * sorted_g[:, None].astype(xn.dtype)
    out = jnp.zeros((T, D), xn.dtype).at[sorted_tok].add(y_slot)
    return out.reshape(B, S, D)

def even_layer(x, norm_mix, w_in, conv_w, conv_b, gate_a_w, gate_a_b, gate_x_w, gate_x_b,
               lam, shift_mu, w0, w_up, a0, a_up, g_up, k_k, k_a, r_k, ln_x_w, ln_x_b,
               w_out, norm_ffn, ffn_w1, ffn_w3, ffn_w2):
    xn = rms_norm(x, norm_mix)
    p = xn @ w_in
    lru_x = p[..., :LRU_WIDTH]
    lru_gate = p[..., LRU_WIDTH:2 * LRU_WIDTH]
    p_rw = p[..., 2 * LRU_WIDTH:]
    xc = causal_dwconv(lru_x, conv_w, conv_b).astype(jnp.float32)
    h = rg_lru(xc, gate_a_w, gate_a_b, gate_x_w, gate_x_b, lam)
    y_lru = h * jax.nn.gelu(lru_gate.astype(jnp.float32), approximate=True)
    y_rw = rwkv7_mix(p_rw, shift_mu, w0, w_up, a0, a_up, g_up, k_k, k_a, r_k, ln_x_w, ln_x_b)
    y = jnp.concatenate([y_lru, y_rw], axis=-1).astype(x.dtype)
    x = x + y @ w_out
    return x + swiglu(rms_norm(x, norm_ffn), ffn_w1, ffn_w3, ffn_w2)

def odd_layer(x, norm_mix, w_in, conv_w, conv_b, wq, wk, wv, ig_b, fg_b, mh_norm_w, w_out,
              norm_ffn, router, moe_w1, moe_w3, moe_w2):
    B, S, _ = x.shape
    xn = rms_norm(x, norm_mix)
    p = xn @ w_in
    x_m = p[..., :MLSTM_WIDTH]
    z = p[..., MLSTM_WIDTH:2 * MLSTM_WIDTH]
    ig_pre = p[..., 2 * MLSTM_WIDTH:2 * MLSTM_WIDTH + MLSTM_HEADS]
    fg_pre = p[..., 2 * MLSTM_WIDTH + MLSTM_HEADS:]
    xc = jax.nn.silu(causal_dwconv(x_m, conv_w, conv_b))
    xch = xc.reshape(B, S, MLSTM_HEADS, MLSTM_HEAD)
    q = jnp.einsum('bshi,hij->bhsj', xch, wq).astype(jnp.float32)
    k = jnp.einsum('bshi,hij->bhsj', xch, wk).astype(jnp.float32)
    v = jnp.einsum('bshi,hij->bhsj', x_m.reshape(B, S, MLSTM_HEADS, MLSTM_HEAD), wv).astype(jnp.float32)
    ig = jnp.moveaxis((ig_pre + ig_b).astype(jnp.float32), 2, 1)
    logf = jnp.moveaxis(jax.nn.log_sigmoid((fg_pre + fg_b).astype(jnp.float32)), 2, 1)
    h = jnp.moveaxis(mlstm_chunkwise(q, k, v, ig, logf), 1, 2)
    h = h * lax.rsqrt(jnp.mean(h * h, axis=-1, keepdims=True) + RMS_EPS)
    h = h.reshape(B, S, MLSTM_WIDTH) * mh_norm_w
    h = jax.nn.sigmoid(z.astype(jnp.float32)) * h
    x = x + h.astype(x.dtype) @ w_out
    return x + moe_swiglu(rms_norm(x, norm_ffn), router, moe_w1, moe_w3, moe_w2)

def setup_inputs(seed: int = 0) -> dict:
    key = jax.random.key(seed)
    ks = iter(jax.random.split(key, 64))
    D = D_MODEL

    def nrm(shape, scale):
        return scale * jax.random.normal(next(ks), shape, jnp.float32)

    def gain(n):
        return 1.0 + nrm((n,), 0.05)

    u = jax.random.uniform(next(ks), (LRU_WIDTH,), jnp.float32, 0.9, 0.999)
    base = u ** (1.0 / LRU_C)
    lam = jnp.log(base) - jnp.log1p(-base)
    return {
        'x': nrm((BATCH, SEQ, D), 1.0),
        'l0_norm_mix': gain(D),
        'l0_w_in': nrm((D, EVEN_IN), D ** -0.5),
        'l0_conv_w': nrm((CONV_WIDTH, LRU_WIDTH), CONV_WIDTH ** -0.5),
        'l0_conv_b': nrm((LRU_WIDTH,), 0.02),
        'l0_gate_a_w': nrm((LRU_BLOCKS, LRU_BLOCK, LRU_BLOCK), LRU_BLOCK ** -0.5),
        'l0_gate_a_b': nrm((LRU_WIDTH,), 0.1),
        'l0_gate_x_w': nrm((LRU_BLOCKS, LRU_BLOCK, LRU_BLOCK), LRU_BLOCK ** -0.5),
        'l0_gate_x_b': nrm((LRU_WIDTH,), 0.1),
        'l0_lru_lambda': lam,
        'l0_shift_mu': jax.random.uniform(next(ks), (EVEN_IN - 2 * LRU_WIDTH,), jnp.float32),
        'l0_w0': jnp.linspace(-6.0, 1.0, RWKV_WIDTH, dtype=jnp.float32) + nrm((RWKV_WIDTH,), 0.1),
        'l0_w_up': nrm((W_LORA, RWKV_WIDTH), 0.1),
        'l0_a0': nrm((RWKV_WIDTH,), 0.1),
        'l0_a_up': nrm((A_LORA, RWKV_WIDTH), 0.1),
        'l0_g_up': nrm((G_LORA, RWKV_WIDTH), G_LORA ** -0.5),
        'l0_k_k': 0.85 + nrm((RWKV_WIDTH,), 0.05),
        'l0_k_a': gain(RWKV_WIDTH),
        'l0_r_k': nrm((RWKV_HEADS, RWKV_HEAD), 0.1),
        'l0_ln_x_w': gain(RWKV_WIDTH),
        'l0_ln_x_b': nrm((RWKV_WIDTH,), 0.02),
        'l0_w_out': nrm((LRU_WIDTH + RWKV_WIDTH, D), (LRU_WIDTH + RWKV_WIDTH) ** -0.5),
        'l0_norm_ffn': gain(D),
        'l0_ffn_w1': nrm((D, D_FF), D ** -0.5),
        'l0_ffn_w3': nrm((D, D_FF), D ** -0.5),
        'l0_ffn_w2': nrm((D_FF, D), D_FF ** -0.5),
        'l1_norm_mix': gain(D),
        'l1_w_in': nrm((D, ODD_IN), D ** -0.5),
        'l1_conv_w': nrm((CONV_WIDTH, MLSTM_WIDTH), CONV_WIDTH ** -0.5),
        'l1_conv_b': nrm((MLSTM_WIDTH,), 0.02),
        'l1_wq': nrm((MLSTM_HEADS, MLSTM_HEAD, MLSTM_HEAD), MLSTM_HEAD ** -0.5),
        'l1_wk': nrm((MLSTM_HEADS, MLSTM_HEAD, MLSTM_HEAD), MLSTM_HEAD ** -0.5),
        'l1_wv': nrm((MLSTM_HEADS, MLSTM_HEAD, MLSTM_HEAD), MLSTM_HEAD ** -0.5),
        'l1_ig_b': nrm((MLSTM_HEADS,), 0.1),
        'l1_fg_b': jnp.linspace(3.0, 6.0, MLSTM_HEADS, dtype=jnp.float32) + nrm((MLSTM_HEADS,), 0.1),
        'l1_mh_norm_w': gain(MLSTM_WIDTH),
        'l1_w_out': nrm((MLSTM_WIDTH, D), MLSTM_WIDTH ** -0.5),
        'l1_norm_ffn': gain(D),
        'l1_router': nrm((D, N_EXPERTS), D ** -0.5),
        'l1_moe_w1': nrm((N_EXPERTS, D, D_FF), D ** -0.5),
        'l1_moe_w3': nrm((N_EXPERTS, D, D_FF), D ** -0.5),
        'l1_moe_w2': nrm((N_EXPERTS, D_FF, D), D_FF ** -0.5),
        'final_norm': gain(D),
    }

def reference(x, l0_norm_mix, l0_w_in, l0_conv_w, l0_conv_b, l0_gate_a_w, l0_gate_a_b,
              l0_gate_x_w, l0_gate_x_b, l0_lru_lambda, l0_shift_mu, l0_w0, l0_w_up, l0_a0,
              l0_a_up, l0_g_up, l0_k_k, l0_k_a, l0_r_k, l0_ln_x_w, l0_ln_x_b, l0_w_out,
              l0_norm_ffn, l0_ffn_w1, l0_ffn_w3, l0_ffn_w2,
              l1_norm_mix, l1_w_in, l1_conv_w, l1_conv_b, l1_wq, l1_wk, l1_wv, l1_ig_b,
              l1_fg_b, l1_mh_norm_w, l1_w_out, l1_norm_ffn, l1_router, l1_moe_w1,
              l1_moe_w3, l1_moe_w2, final_norm):
    layer_params = [
        (l0_norm_mix, l0_w_in, l0_conv_w, l0_conv_b, l0_gate_a_w, l0_gate_a_b, l0_gate_x_w,
         l0_gate_x_b, l0_lru_lambda, l0_shift_mu, l0_w0, l0_w_up, l0_a0, l0_a_up, l0_g_up,
         l0_k_k, l0_k_a, l0_r_k, l0_ln_x_w, l0_ln_x_b, l0_w_out, l0_norm_ffn, l0_ffn_w1,
         l0_ffn_w3, l0_ffn_w2),
        (l1_norm_mix, l1_w_in, l1_conv_w, l1_conv_b, l1_wq, l1_wk, l1_wv, l1_ig_b, l1_fg_b,
         l1_mh_norm_w, l1_w_out, l1_norm_ffn, l1_router, l1_moe_w1, l1_moe_w3, l1_moe_w2),
    ]
    for layer in range(DEPTH):
        if layer % 2 == 0:
            x = even_layer(x, *layer_params[layer])
        else:
            x = odd_layer(x, *layer_params[layer])
    return rms_norm(x, final_norm)


_drawn_inputs = setup_inputs


def setup_inputs(seed=0):
    import zlib

    import numpy as np

    out = dict(_drawn_inputs(seed))
    spreads = {}
    factors = {'l1_conv_b': 3.163, 'l1_ig_b': 64.0}
    for name, (base, spread) in spreads.items():
        noise = np.random.default_rng([zlib.crc32(name.encode()), seed]).standard_normal(out[name].shape)
        drawn = base * np.exp(spread * noise) if base else spread * noise
        out[name] = __import__('jax').numpy.asarray(drawn.astype(out[name].dtype))
    for name, factor in factors.items():
        out[name] = (out[name] * factor).astype(out[name].dtype)
    return out
```

```python
from contextlib import ExitStack

import numpy as np

import concourse.bass as bass
from concourse import mybir

ALU = mybir.AluOpType
ACT = mybir.ActivationFunctionType
AX = mybir.AxisListType
F32 = mybir.dt.float32
I32 = mybir.dt.int32
U32 = mybir.dt.uint32
U8 = mybir.dt.uint8

P = 128
T = 256
D = 1024
KD = D // P
CH = T // P
F = 2816
NF = F // P
RS = NF // 2
GROUPS = [(0, 4), (4, 8), (8, 11)]
E = 8
HD = 64
LV = 7
DECAY = float(np.exp(-0.5))
SLOTS = 96
PASSES = -(-T // SLOTS)

VECS = {}
NV = 0
for _name, _n in [("l0_norm_mix", 8), ("l0_conv_w", 16), ("l0_conv_b", 4), ("l0_gate_a_b", 4),
                  ("l0_gate_x_b", 4), ("l0_lru_lambda", 4), ("l0_shift_mu", 14), ("l0_w0", 4),
                  ("l0_a0", 4), ("l0_k_k", 4), ("l0_k_a", 4), ("l0_r_k", 4), ("l0_ln_x_w", 4),
                  ("l0_ln_x_b", 4), ("l0_norm_ffn", 8), ("l1_norm_mix", 8), ("l1_conv_w", 32),
                  ("l1_conv_b", 8), ("l1_mh_norm_w", 8), ("l1_norm_ffn", 8), ("final_norm", 8)]:
    VECS[_name] = NV
    NV += _n

IDENT, BLK, ONES, MEAN_D, MEAN_H, BLKM, SU, IU, SL, IOTA, ROWS, EPS = [P * i for i in range(12)]
NCONST = EPS + 2


def constants():
    s, t = np.arange(P)[:, None], np.arange(P)[None, :]
    c = np.zeros((P, NCONST), np.float32)
    c[:, IDENT:IDENT + P] = s == t
    c[:, BLK:BLK + P] = s // HD == t // HD
    c[:, ONES:ONES + P] = 1.0
    c[:, MEAN_D:MEAN_D + P] = 1.0 / D
    c[:, MEAN_H:MEAN_H + P] = 1.0 / P
    c[:, BLKM:BLKM + P] = (s // HD == t // HD) / HD
    c[:, SU:SU + P] = s < t
    c[:, IU:IU + P] = s <= t
    c[:, SL:SL + P] = t < s
    c[:, IOTA:IOTA + P] = t
    c[:, ROWS:ROWS + P] = np.concatenate([np.arange(32), np.arange(64, 96), np.arange(32, 64), np.arange(32, 64)])
    c[:, EPS] = 1e-6
    c[:, EPS + 1] = 1e-5 * HD
    m = np.zeros((P, 2, LV, P), np.float32)
    for lv in range(LV):
        b = 1 << lv
        m[:, 0, lv] = (s // (2 * b) == t // (2 * b)) & ((s // b) % 2 == 0) & ((t // b) % 2 == 1)
        m[:, 1, lv] = m[:, 0, lv].T
    sel = np.zeros((8, 8, P), np.float32)
    sel[np.arange(8), np.arange(8)] = 1.0
    return c, m.reshape(P, 2 * LV * P), sel.reshape(8, 8 * P)


def hybrid_rglru_rwkv7_mlstm_moe(nc, A, out):
    ctx = ExitStack()
    with ctx:
        def sb(name, shape, dt=F32):
            return ctx.enter_context(nc.sbuf_tensor(name, shape, dt))

        def sem(name):
            return ctx.enter_context(nc.semaphore(name))

        REG = RS * D
        W = sb("W", [P, 3 * REG])
        RA, RB, RC = 0, REG, 2 * REG
        x = sb("x", [P, KD, T])
        xn = sb("xn", [P, KD, T])
        SN = 12900
        S = sb("S", [P, SN])
        cf = sb("cf", [P, NCONST])
        lm = sb("lm", [P, 2 * LV * P], U8)
        vec = sb("vec", [P, NV])
        misc = sb("misc", [P, 96])
        rs = sb("rs", [P, T])
        ps = ctx.enter_context(nc.psum_tensor("ps", [P, 8, 512], F32))

        def view(buf, start, pattern, /, **dims):
            n = 1
            for v in dims.values():
                n *= v
            return buf[:, start:start + n].rearrange(pattern, **dims)

        def col(name, j):
            return vec[:, VECS[name] + j:VECS[name] + j + 1]

        def con(at, rows=slice(0, P), n=P):
            return cf[rows, at:at + n]

        WIN_BLOCKS = [(20, 2), (12, 4), (8, 4), (16, 4), (0, 4), (4, 4)]
        win = []
        at = RA
        for j0, n in WIN_BLOCKS:
            win.append(view(W, at, "p (k n) -> p k n", k=KD, n=n * P))
            at += KD * n * P
        wo0 = view(W, RC, "p (k n) -> p k n", k=KD, n=D)
        small0 = W[:, RC + KD * D:RC + KD * D + 2048]
        gate_a = view(small0, 0, "p (j n) -> p j n", j=4, n=P)
        gate_x = view(small0, 512, "p (j n) -> p j n", j=4, n=P)
        lora_up = view(small0, 1024, "p (j n) -> p j n", j=4, n=P)
        g_up = view(small0, 1536, "p (j n) -> p j n", j=4, n=P)
        at = 0

        def take(n):
            nonlocal at
            at += n
            assert at <= SN
            return at - n

        mix = view(S, take(14 * T), "p (j t) -> p j t", j=14, t=T)
        r_, k_, v_ = mix[:, 0:4], mix[:, 4:8], mix[:, 8:12]
        AR = view(S, take(2048), "p (c j a t) -> p c j a t", c=CH, j=4, a=2, t=P)
        lmf = S[:, at - 2048:at - 2048 + 2 * LV * P]
        Bm = view(S, take(1024), "p (c j t) -> p c j t", c=CH, j=4, t=P)
        Kt = view(S, take(1024), "p (c j t) -> p c j t", c=CH, j=4, t=P)
        rk = view(S, take(1024), "p (j t) -> p j t", j=4, t=T)
        gate_rw = view(S, take(1024), "p (j t) -> p j t", j=4, t=T)
        lxp = view(S, take(4 * 259), "p (j t) -> p j t", j=4, t=259)
        gelu = view(S, take(1024), "p (j t) -> p j t", j=4, t=T)
        KB = RA + 2048
        Em = view(W, KB, "p (j c t) -> p j c t", j=4, c=CH, t=P)
        a_ = view(W, KB + 1024, "p (j t) -> p j t", j=4, t=T)
        kk = view(W, KB + 2048, "p (j t) -> p j t", j=4, t=T)
        tmp = view(W, KB + 3072, "p (j t) -> p j t", j=4, t=T)
        Gp = view(W, KB + 4096, "p (j c t) -> p j c t", j=4, c=CH, t=P + 1)
        Ep = view(W, KB + 4096 + 1032, "p (j c t) -> p j c t", j=4, c=CH, t=P + 1)
        sg = view(W, KB + 4096 + 2064, "p (j t) -> p j t", j=4, t=T)
        NR = view(W, KB, "p (q j a t) -> p q j a t", q=4, j=4, a=2, t=P)
        RBt = view(W, KB + 4096, "p (q j t) -> p q j t", q=4, j=4, t=P)
        XT = view(W, KB + 6144, "p (q j t) -> p q j t", q=4, j=4, t=P)
        M = view(W, KB + 8192, "p (q j t) -> p q j t", q=4, j=4, t=P)
        Z = view(W, KB + 10240, "p (q j t) -> p q j t", q=4, j=4, t=P)
        XB = KB + 12288
        Vt = view(W, XB, "p (c j v) -> p c j v", c=CH, j=4, v=P)
        Bt = view(W, XB + 1024, "p (c j v) -> p c j v", c=CH, j=4, v=P)
        Ktk = view(W, XB + 2048, "p (c j v) -> p c j v", c=CH, j=4, v=P)
        U = view(W, XB + 6144, "p (c h v) -> p c h v", c=CH, h=8, v=HD)
        lr = view(W, XB + 4096, "p (j t) -> p j t", j=4, t=T)
        li = view(W, XB + 5120, "p (j t) -> p j t", j=4, t=T)
        xc0 = view(W, XB + 3072, "p (j t) -> p j t", j=4, t=T)
        lt = view(W, XB + 7168, "p (j t) -> p j t", j=4, t=T)
        X = view(W, RA, "p (q j t) -> p q j t", q=4, j=4, t=P)
        y0 = view(W, RA, "p (j c t) -> p j c t", j=4, c=CH, t=P)
        y0f = view(W, RA, "p (j t) -> p j t", j=4, t=T)
        y1f = view(W, RA + 1024, "p (j t) -> p j t", j=4, t=T)
        RHS = view(W, KB + 10240, "p (c h v) -> p c h v", c=CH, h=8, v=HD)
        ST = view(W, KB + 11264, "p (j v) -> p j v", j=4, v=HD)
        SP4, SPM = misc[:, 0:4], misc[:, 4:8]
        OMM = misc[:, 48:62]
        OKA = misc[:, 62:66]
        CPOS, CNEG = misc[:, 66:74], misc[:, 74:82]
        DSC = misc[:, 82:86]

        w1r = view(W, RA, "p (k n) -> p k n", k=KD, n=RS * P)
        w3r = view(W, RB, "p (k n) -> p k n", k=KD, n=RS * P)
        w2r = view(W, RC, "p (s n) -> p s n", s=RS, n=D)
        sil0 = view(S, 0, "p (b t) -> p b t", b=4, t=T)
        hid0 = view(S, 1024, "p (b t) -> p b t", b=4, t=T)
        wxm = view(W, RA, "p (k n) -> p k n", k=KD, n=D)
        wgt = view(W, RA + KD * D, "p (k n) -> p k n", k=KD, n=16)
        sel = W[0:8, RA + KD * D + 128:RA + KD * D + 128 + 8 * P].rearrange("p (h n) -> p h n", h=8)
        wz = view(W, RB, "p (k n) -> p k n", k=KD, n=D)
        wo1 = view(W, RC, "p (k n) -> p k n", k=KD, n=D)
        wqkv = view(W, RC + KD * D, "p (a h n) -> p a h n", a=3, h=8, n=P)
        q1 = view(W, RA, "p (h t) -> p h t", h=8, t=T)
        k1 = view(W, RA + 2048, "p (h t) -> p h t", h=8, t=T)
        kt1 = view(W, RA + 4096, "p (h c d) -> p h c d", h=8, c=CH, d=P)
        vt1 = view(W, RA + 6144, "p (h c d) -> p h c d", h=8, c=CH, d=P)
        at = 0
        xmp = view(S, take(8 * 259), "p (j t) -> p j t", j=8, t=259)
        zs = view(S, take(2048), "p (j t) -> p j t", j=8, t=T)
        xc1 = view(S, take(2048), "p (j t) -> p j t", j=8, t=T)
        dlog = view(S, take(512), "p (b t) -> p b t", b=2, t=T)
        dmat = view(S, take(512), "p (b t) -> p b t", b=2, t=T)
        sT = view(S, take(512), "p (b t) -> p b t", b=2, t=T)
        enm = view(S, take(512), "p (b t) -> p b t", b=2, t=T)
        CN = view(S, take(512), "p (b t) -> p b t", b=2, t=T)
        kw = view(S, take(256), "p (b t) -> p b t", b=2, t=P)
        qsc = view(S, take(256), "p (b t) -> p b t", b=2, t=P)
        den = view(S, take(512), "p (b t) -> p b t", b=2, t=T)
        wts = S[:, take(8):][:, 0:8]
        gtok = view(S, take(16), "p (c h) -> p c h", c=CH, h=8)
        at0 = take(10 * T)
        row = S[0:8, at0:at0 + 10 * T].rearrange("p (n t) -> p n t", n=10)
        h1 = xn
        at = 0
        xtok = view(S, take(2048), "p (c n) -> p c n", c=CH, n=D)
        OH = view(S, take(9 * T), "p (e c s) -> p e c s", e=9, c=CH, s=SLOTS)
        SG = view(S, take(9 * T), "p (e t) -> p e t", e=9, t=T)
        OHg = view(S, take(2 * T), "p (b c s) -> p b c s", b=2, c=CH, s=P)
        xg = view(S, take(2 * KD * SLOTS), "p (b k s) -> p b k s", b=2, k=KD, s=SLOTS)
        sil = view(S, take(2 * T), "p (b n) -> p b n", b=2, n=2 * SLOTS)
        hid = view(S, take(4 * T), "p (b f s) -> p b f s", b=4, f=2, s=SLOTS)
        ye = S[:, take(D):][:, 0:D]
        at0 = take(8 * 16)
        rt = S[:, at0:at0 + 128].rearrange("p (n e) -> p n e", n=16)
        wrt = view(S, take(64), "p (k e) -> p k e", k=KD, e=E)
        gb = sb("gb", [8, 2])
        idx = sb("idx", [P, CH, 8], U32)
        flag = sb("flag", [1, 1], I32)

        in_x, in_con, in_late = sem("in_x"), sem("in_con"), sem("in_late")
        in_win = [sem(f"in_win{i}") for i in range(6)]
        in_small0, in_wo0 = sem("in_small0"), sem("in_wo0")
        in_w1 = [sem(f"in_w1_{g}") for g in range(3)]
        in_w3 = [sem(f"in_w3_{g}") for g in range(3)]
        in_w2 = [sem(f"in_w2_{g}") for g in range(3)]
        in_xm, in_z, in_qkv, in_wo1, in_rt = sem("in_xm"), sem("in_z"), sem("in_qkv"), sem("in_wo1"), sem("in_rt")
        stored = sem("stored")
        dve_seq, act_seq, pool_seq = sem("dve_seq"), sem("act_seq"), sem("pool_seq")
        sq_done, mean_done, root_done, xn_done = sem("sq_done"), sem("mean_done"), sem("root_done"), sem("xn_done")
        zeroed = sem("zeroed")
        proj, part, mixed, lgact = sem("proj"), sem("part"), sem("mixed"), sem("lgact")
        omm_done, lora_act, kk_sq, kk_sum, kk_root, kk_ready = [sem(n) for n in
            ("omm_done", "lora_act", "kk_sq", "kk_sum", "kk_root", "kk_ready")]
        z_done, sg_done, am_done, a_done, g_done, g_out, cum_done, e_done = [sem(n) for n in
            ("z_done", "sg_done", "am_done", "a_done", "g_done", "g_out", "cum_done", "e_done")]
        lam_exp, lam_in, sp4_done = sem("lam_exp"), sem("lam_in"), sem("sp4_done")
        conv0, lgate, lgate_out, lth, lth_in, lroot, y_lru = [sem(n) for n in
            ("conv0", "lgate", "lgate_out", "lth", "lth_in", "lroot", "y_lru")]
        ops_done, tr_done, tr_out, pair_done, pair_out, xt_init = [sem(n) for n in
            ("ops_done", "tr_done", "tr_out", "pair_done", "pair_out", "xt_init")]
        zmm, zcp, xmm, xcp = sem("zmm"), sem("zcp"), sem("xmm"), sem("xcp")
        nv_done, nv_out, u_done, u_out, st_done, st_out, y_done, y_out = [sem(n) for n in
            ("nv_done", "nv_out", "u_done", "u_out", "st_done", "st_out", "y_done", "y_out")]
        ln_mm, ln_c, ln_sq, ln_root, bonus_mm, y_rw = [sem(n) for n in
            ("ln_mm", "ln_c", "ln_sq", "ln_root", "bonus_mm", "y_rw")]
        wo_done, res_done = sem("wo_done"), sem("res_done")
        up_done, silu_done, hid_done, down_done = [sem(n) for n in ("up_done", "silu_done", "hid_done", "down_done")]
        gt_done, p1, rows_in, row_g, row_m, rows_done, gtr_done, gtok_out = [sem(n) for n in
            ("gt_done", "p1", "rows_in", "row_g", "row_m", "rows_done", "gtr_done", "gtok_out")]
        xm_out, z_out, conv1, xc_done, qkv_done, qk_out, kv_out = [sem(n) for n in
            ("xm_out", "z_out", "conv1", "xc_done", "qkv_done", "qk_out", "kv_out")]
        bc_done, kq_done, dlog_done, exp_done, masked, wts_done, enm_out, qsc_done, kw_done = [sem(n) for n in
            ("bc_done", "kq_done", "dlog_done", "exp_done", "masked", "wts_done", "enm_out", "qsc_done", "kw_done")]
        cn_done, cn_out, sT_done, nd_done, h_done, hsq_done, hm_done, hroot_done, y1_done = [sem(n) for n in
            ("cn_done", "cn_out", "sT_done", "nd_done", "h_done", "hsq_done", "hm_done", "hroot_done", "y1_done")]
        lg_done, tk_done, tk_out, rt_exp_in, rt_exp, sel_done, pos_done, pos_out, slots_done, flag_done = [sem(n) for n in
            ("lg_done", "tk_done", "tk_out", "rt_exp_in", "rt_exp", "sel_done", "pos_done", "pos_out", "slots_done", "flag_done")]
        oh_done, ohg_done, sgt_done, sg_out, moe_zero = [sem(n) for n in
            ("oh_done", "ohg_done", "sgt_done", "sg_out", "moe_zero")]
        m_up, m_silu, m_hid, m_down, m_yout, m_sc, m_add, m_gather, m_xg = [sem(n) for n in
            ("m_up", "m_silu", "m_hid", "m_down", "m_yout", "m_sc", "m_add", "m_gather", "m_xg")]
        lm_ready = sem("lm_ready")
        x_final, pos_shifted = sem("x_final"), sem("pos_shifted")

        SQ = {"mix0": 0, "ffn0": 1, "mix1": 2, "ffn1": 3, "final": 4}

        block = ctx.enter_context(nc.Block())

        PAIRS = []
        for b, (j0, n) in enumerate(WIN_BLOCKS):
            for i in range(0, n, 2):
                PAIRS.append((b, i * P, j0 + i))
        MIXAT = {8 + i: i for i in range(4)} | {12 + i: 4 + i for i in range(4)} | {16 + i: 8 + i for i in range(4)} | {20: 12, 21: 13}

        def half(i):
            return slice(HD * i, HD * i + HD)

        @block.sync
        def _(sp):
            sp.dma_start(x[:, :, :], A["xT"].rearrange("(k p) t -> p k t", p=P)).then_inc(in_x, 16)
            sp.dma_start(cf[:, :], A["cf"]).then_inc(in_con, 16)
            w = A["l0_w_in"].rearrange("(k p) n -> p k n", p=P)
            for b, (j0, n) in enumerate(WIN_BLOCKS):
                sp.dma_start(win[b], w[:, :, j0 * P:(j0 + n) * P]).then_inc(in_win[b], 16)
                if b == 1:
                    sp.dma_start(small0, A["small0"]).then_inc(in_small0, 16)
            sp.dma_start(wo0, A["l0_w_out"].rearrange("(k p) n -> p k n", p=P)).then_inc(in_wo0, 16)

            def ring(w1, w3, w2, h, wait13, wait2):
                for g, (s0, s1) in enumerate(GROUPS):
                    c0, c1 = (RS * h + s0) * P, (RS * h + s1) * P
                    wait13(g)
                    sp.dma_start(w1r[:, :, s0 * P:s1 * P], w1[:, :, c0:c1]).then_inc(in_w1[g], 16)
                    sp.dma_start(w3r[:, :, s0 * P:s1 * P], w3[:, :, c0:c1]).then_inc(in_w3[g], 16)
                    wait2(g)
                    sp.dma_start(w2r[:, s0:s1, :], w2[:, RS * h + s0:RS * h + s1, :]).then_inc(in_w2[g], 16)

            f1 = A["l0_ffn_w1"].rearrange("(k p) n -> p k n", p=P)
            f3 = A["l0_ffn_w3"].rearrange("(k p) n -> p k n", p=P)
            f2 = A["l0_ffn_w2"].rearrange("(s p) n -> p s n", p=P)
            sp.wait_ge(y_lru, 1)
            sp.wait_ge(y_rw, 2)
            ring(f1, f3, f2, 0, lambda g: None,
                 lambda g: sp.wait_ge(wo_done, 4) if g == 0 else None)
            ring(f1, f3, f2, 1, lambda g: sp.wait_ge(up_done, GROUPS[g][1]),
                 lambda g: sp.wait_ge(down_done, GROUPS[g][1]))

            w = A["l1_w_in"].rearrange("(k p) n -> p k n", p=P)
            sp.wait_ge(up_done, NF)
            sp.dma_start(wgt, A["wgt"].rearrange("p (k n) -> p k n", k=KD)).then_inc(in_xm, 16)
            sp.dma_start(sel, A["sel"].rearrange("p (h n) -> p h n", h=8)).then_inc(in_xm, 16)
            sp.dma_start(wxm, w[:, :, 0:D]).then_inc(in_xm, 16)
            sp.dma_start(wz, w[:, :, D:2 * D]).then_inc(in_z, 16)
            sp.wait_ge(down_done, NF)
            sp.dma_start(wqkv, A["wqkv"].rearrange("p (a h n) -> p a h n", a=3, h=8)).then_inc(in_qkv, 16)
            sp.dma_start(wo1, A["l1_w_out"].rearrange("(k p) n -> p k n", p=P)).then_inc(in_wo1, 16)

            e1 = A["l1_moe_w1"].rearrange("e (k p) n -> e p k n", p=P)
            e3 = A["l1_moe_w3"].rearrange("e (k p) n -> e p k n", p=P)
            e2 = A["l1_moe_w2"].rearrange("e (s p) n -> e p s n", p=P)
            sp.wait_ge(res_done, 24)
            sp.dma_start(wrt, A["wrt"].rearrange("p (k e) -> p k e", k=KD)).then_inc(in_rt, 16)

            def load13(g, e, h, w, dst, s):
                s0, s1 = GROUPS[g]
                sp.dma_start(dst[:, :, s0 * P:s1 * P], w[e, :, :, (RS * h + s0) * P:(RS * h + s1) * P]).then_inc(s[g], 16)

            def load2(g, e, h):
                s0, s1 = GROUPS[g]
                sp.dma_start(w2r[:, s0:s1, :], e2[e, :, RS * h + s0:RS * h + s1, :]).then_inc(in_w2[g], 16)

            def half0(e, ge, first):
                for g in range(3):
                    if not first:
                        sp.wait_ge(m_up, ge * RS + (8, 10, 11)[g])
                    load13(g, e, 0, e1, w1r, in_w1)
                    load13(g, e, 0, e3, w3r, in_w3)
                    if not first:
                        sp.wait_ge(m_down, ge * RS + (8, 10, 11)[g])
                    load2(g, e, 0)

            def half1(e, ge):
                for g in range(3):
                    sp.wait_ge(m_up, ge * RS + RS + (2, 4, 6)[g])
                    load13(g, e, 1, e1, w1r, in_w1)
                    load13(g, e, 1, e3, w3r, in_w3)
                    sp.wait_ge(m_down, ge * RS + RS + (2, 4, 6)[g])
                    load2(g, e, 1)

            sp.wait_ge(wo_done, 8)
            half0(0, 0, True)
            with sp.Fori(0, E - 1) as e:
                half1(e, e)
                half0(e + 1, e + 1, False)
            half1(E - 1, E - 1)
            sp.wait_ge(flag_done, 1)
            over = sp.value_load(flag[0:1, 0:1], min_val=0, max_val=1)
            with sp.If(over != 0):
                for n in range(1, PASSES):
                    half0(0, E * n, False)
                    with sp.Fori(0, E - 1) as e:
                        half1(e, e + E * n)
                        half0(e + 1, e + (E * n + 1), False)
                    half1(E - 1, E * n + E - 1)

            for k in range(KD):
                sp.wait_ge(xn_done, 4 * KD + k + 1)
                sp.dma_start(out[k * P:(k + 1) * P, :], xn[:, k, :]).then_inc(stored, 16)
            sp.wait_ge(stored, 16 * KD)

        @block.gpsimd
        def _(pool):
            n = [0]

            def step(ins):
                n[0] += 1
                ins.then_inc(pool_seq, 1)
                pool.wait_ge(pool_seq, n[0])

            nc.gpsimd.memset(lxp[:, :, 0:3], 0.0).then_inc(zeroed, 1)
            pool.wait_ge(in_con, 32)
            pool.wait_ge(in_late, 32)
            nc.gpsimd.tensor_copy(lm[:, :], lmf).then_inc(lm_ready, 1)
            pool.wait_ge(ops_done, 1)
            for q in range(4):
                ins = nc.gpsimd.tensor_copy(XT[:, q], con(IDENT).unsqueeze(1).broadcast_to([P, 4, P]))
                ins = nc.gpsimd.tensor_copy(X[:, q], con(IDENT).unsqueeze(1).broadcast_to([P, 4, P]))
                ins.then_inc(xt_init, 1)
            pool.wait_ge(res_done, 16)
            nc.gpsimd.memset(xmp[:, :, 0:3], 0.0).then_inc(zeroed, 1)
            for h in range(8):
                pool.wait_ge(exp_done, h + 1)
                b = h % 2
                nc.gpsimd.tensor_tensor(dmat[:, b, :].rearrange("p (c t) -> p c t", c=CH), dmat[:, b, :].rearrange("p (c t) -> p c t", c=CH),
                                        con(IU).unsqueeze(1).broadcast_to([P, CH, P]), ALU.mult).then_inc(masked, 1)
            pool.wait_ge(res_done, 24)
            nc.gpsimd.memset(OH[:, E, :, :], 0.0).then_inc(moe_zero, 1)
            nc.gpsimd.memset(SG[:, 0, :], 0.0).then_inc(moe_zero, 1)
            nc.gpsimd.memset(ye, 0.0).then_inc(m_yout, 1)
            for s in (m_up, m_hid, m_down):
                pool.sem_inc(s, RS)

        @block.tensor
        def _(pe):
            def mm(o, l, r, start, stop, **kw):
                return nc.tensor.matmul(o, l, r, start=start, stop=stop, **kw)

            def norm_mean(i, bank):
                for k in range(KD):
                    pe.wait_ge(sq_done, KD * i + k + 1)
                    ins = mm(ps[:, bank, 0:T], con(MEAN_D), xn[:, k, :], k == 0, k == KD - 1)
                ins.then_inc(mean_done, 1)

            pe.wait_ge(in_con, 32)
            norm_mean(0, 4)

            def project(i):
                b, c0, j = PAIRS[i]
                if c0 == 0:
                    pe.wait_ge(in_win[b], 16)
                if i >= 4:
                    if i - 4 < 7:
                        pe.wait_ge(mixed, 2 * (i - 3))
                    else:
                        pe.wait_ge(lgact, 2 * (i - 3 - 7))
                for u in range(2):
                    for k in range(KD):
                        if i == 0 and u == 0:
                            pe.wait_ge(xn_done, k + 1)
                        ins = mm(ps[:, i % 4, u * T:(u + 1) * T], win[b][:, k, c0 + u * P:c0 + (u + 1) * P],
                                 xn[:, k, :], k == 0, k == KD - 1)
                ins.then_inc(proj, 1)

            project(0)
            project(1)
            project(2)
            pe.wait_ge(in_small0, 16)
            pe.wait_ge(lora_act, 1)
            for j in range(4):
                ins = mm(ps[:, 6 + j // 2, (j % 2) * T:(j % 2 + 1) * T], lora_up[0:HD, j, :], mix[0:HD, 12, :], True, True)
            ins.then_inc(z_done, 1)
            project(3)
            pe.wait_ge(kk_sq, 1)
            pe.wait_ge(root_done, 1)
            for i in range(2):
                ins = mm(ps[:, 4 + i, :], con(BLK), tmp[:, 2 * i:2 * i + 2, :].rearrange("p j t -> p (j t)"), True, True)
            ins.then_inc(kk_sum, 1)
            project(4)
            pe.wait_ge(sg_done, 1)
            for j in range(4):
                ins = mm(ps[:, 6 + j // 2, (j % 2) * T:(j % 2 + 1) * T], lora_up[HD:P, j, :], mix[HD:P, 12, :], True, True)
            ins.then_inc(am_done, 1)
            project(5)
            project(6)
            pe.wait_ge(kk_root, 1)
            pe.wait_ge(lora_act, 2)
            for j in range(4):
                ins = mm(ps[:, 4 + j // 2, (j % 2) * T:(j % 2 + 1) * T], g_up[:, j, :], mix[:, 13, :], True, True)
            ins.then_inc(g_done, 1)
            for i in range(7, 11):
                project(i)

            pe.wait_ge(mixed, 14)
            unit = 0

            def transposed(src):
                nonlocal unit
                for c in range(CH):
                    if unit == 0:
                        pe.wait_ge(a_done, 1)
                        pe.wait_ge(g_out, 1)
                    if unit >= 4:
                        pe.wait_ge(tr_out, unit - 3)
                    for j in range(4):
                        ins = nc.tensor.transpose(ps[:, 4 + unit % 4, j * P:(j + 1) * P], src(c, j), con(IDENT))
                    ins.then_inc(tr_done, 1)
                    unit += 1

            transposed(lambda c, j: v_[:, j, c * P:(c + 1) * P])
            pe.wait_ge(conv0, 1)
            pe.wait_ge(lgact, 8)
            for a, g in enumerate((gate_a, gate_x)):
                for j in range(4):
                    ins = mm(ps[:, 2 * a + j // 2, (j % 2) * T:(j % 2 + 1) * T], g[:, j, :], xc0[:, j, :], True, True)
                ins.then_inc(lgate, 1)
            pe.wait_ge(ops_done, 1)
            transposed(lambda c, j: Bm[:, c, j, :])
            transposed(lambda c, j: Kt[:, c, j, :])

            pe.wait_ge(lgate_out, 2)
            pe.wait_ge(tr_out, 6)
            unit = 0

            def claim(n):
                nonlocal unit
                pe.wait_ge(pair_out, max(unit + n - 8, 0)) if unit + n > 8 else None
                banks = [(unit + i) % 8 for i in range(n)]
                unit += n
                return banks

            for q in range(4):
                c, h = q // 2, half(q % 2)
                for left in (Kt, Bm):
                    banks = claim(2)
                    for j in range(4):
                        ins = mm(ps[:, banks[j // 2], (j % 2) * T:(j % 2 + 1) * T], left[h, c, j, :],
                                 AR[h, c, j, :, :].rearrange("p a t -> p (a t)"), True, True)
                    ins.then_inc(pair_done, 1)
                bank, = claim(1)
                for j in range(4):
                    ins = mm(ps[:, bank, j * P:(j + 1) * P], AR[h, c, j, 0, :], Bm[h, c, j, :], True, True)
                ins.then_inc(pair_done, 1)

            pe.wait_ge(pair_out, 20)
            for lv in range(1, LV):
                for q in range(4):
                    if lv > 1:
                        pe.wait_ge(xcp, 4 * (lv - 2) + q + 1)
                    for j in range(4):
                        ins = mm(ps[:, q, j * P:(j + 1) * P], M[:, q, j, :], XT[:, q, j, :], True, True)
                    ins.then_inc(zmm, 1)
                for q in range(4):
                    pe.wait_ge(zcp, 4 * (lv - 1) + q + 1)
                    for j in range(4):
                        ins = mm(ps[:, 4 + q, j * P:(j + 1) * P], X[:, q, j, :], Z[:, q, j, :], True, True)
                    if lv < LV - 1:
                        for j in range(4):
                            ins = mm(ps[:, q, j * P:(j + 1) * P], Z[:, q, j, :], X[:, q, j, :], True, True)
                    ins.then_inc(xmm, 1)

            for c in range(CH):
                if c == 1:
                    pe.wait_ge(st_out, 1)
                for hh in range(8):
                    q, j = 2 * c + hh % 2, hh // 2
                    bank = 0 if c == 0 or hh % 2 else 1
                    ins = mm(ps[:, bank, hh * HD:(hh + 1) * HD], NR[:, q, j, 0, :],
                             Vt[:, c, j, half(hh % 2)], True, c == 0)
                    if c == 1:
                        ins = mm(ps[:, bank, hh * HD:(hh + 1) * HD], AR[half(hh % 2), c, j, 0, :],
                                 ST[half(hh % 2), j, :], False, True)
                ins.then_inc(nv_done, 1)
                pe.wait_ge(nv_out, c + 1)
                if c == 0:
                    pe.wait_ge(xcp, 4 * (LV - 1))
                for hh in range(8):
                    ins = mm(ps[:, 2, hh * HD:(hh + 1) * HD], XT[:, 2 * c + hh % 2, hh // 2, :], RHS[:, c, hh, :], True, True)
                ins.then_inc(u_done, 1)
                pe.wait_ge(u_out, c + 1)
                if c == 0:
                    for hh in range(8):
                        j, h = hh // 2, half(hh % 2)
                        mm(ps[h, 3, j * HD:(j + 1) * HD], Bt[:, 0, j, h], U[:, 0, hh, :], True, False)
                        ins = mm(ps[h, 3, j * HD:(j + 1) * HD], Ktk[:, 0, j, h], Vt[:, 0, j, h], False, True)
                    ins.then_inc(st_done, 1)
                for par in range(2):
                    for j in range(4):
                        h, q = half(par), 2 * c + par
                        o = ps[h, 4 + 2 * par + c, j * P:(j + 1) * P]
                        mm(o, Vt[:, c, j, h], NR[:, q, j, 1, :], True, False)
                        ins = mm(o, U[:, c, 2 * j + par, :], RBt[:, q, j, :], False, c == 0)
                        if c == 1:
                            ins = mm(o, ST[h, j, :], AR[h, c, j, 1, :], False, True)
                ins.then_inc(y_done, 1)

            def project_out(w, ds, ks):
                for d in ds:
                    for k in ks:
                        ins = mm(ps[:, d // 2, (d % 2) * T:(d % 2 + 1) * T], w[:, k, d * P:(d + 1) * P],
                                 xn[:, k, :], k == 0 and d % 2 == 0, k == KD - 1, skip_group_check=True)
                    if d % 2 and ks[-1] == KD - 1:
                        ins.then_inc(wo_done, 1)

            pe.wait_ge(in_wo0, 16)
            pe.wait_ge(y_lru, 1)
            pe.wait_ge(st_out, 1)
            project_out(wo0, range(0, 2), range(4))
            pe.wait_ge(y_out, 4)
            for i in range(2):
                ins = mm(ps[:, 4 + i, :], con(BLKM), y0f[:, 2 * i:2 * i + 2, :].rearrange("p j t -> p (j t)"), True, True)
            ins.then_inc(ln_mm, 1)
            for i in range(2):
                ins = mm(ps[:, 6 + i, :], con(BLK), rk[:, 2 * i:2 * i + 2, :].rearrange("p j t -> p (j t)"), True, True)
            ins.then_inc(bonus_mm, 1)
            project_out(wo0, range(2, 5), range(4))
            pe.wait_ge(ln_sq, 1)
            for i in range(2):
                ins = mm(ps[:, 4 + i, :], con(BLKM), y0f[:, 2 * i:2 * i + 2, :].rearrange("p j t -> p (j t)"), True, True)
            ins.then_inc(ln_mm, 1)

            project_out(wo0, range(5, KD), range(4))
            for i in range(2):
                pe.wait_ge(y_rw, i + 1)
                project_out(wo0, range(KD), range(4 + 2 * i, 6 + 2 * i))

            norm_mean(1, 4)
            pe.wait_ge(root_done, 2)

            def up(f):
                h, s = divmod(f, RS)
                g = min(s // 4, 2)
                if s % 4 == 0:
                    pe.wait_ge(in_w1[g], 16 * (h + 1))
                    pe.wait_ge(in_w3[g], 16 * (h + 1))
                if f >= 4:
                    pe.wait_ge(hid_done, f - 3)
                for a, w in enumerate((w1r, w3r)):
                    for k in range(KD):
                        if f == 0 and a == 0:
                            pe.wait_ge(xn_done, KD + k + 1)
                        ins = mm(ps[:, 4 + f % 4, a * T:(a + 1) * T], w[:, k, s * P:(s + 1) * P], xn[:, k, :],
                                 k == 0, k == KD - 1)
                ins.then_inc(up_done, 1)

            def down(f):
                h, s = divmod(f, RS)
                if s % 4 == 0:
                    pe.wait_ge(in_w2[min(s // 4, 2)], 16 * (h + 1))
                pe.wait_ge(hid_done, f + 1)
                for d in range(KD):
                    ins = mm(ps[:, d // 2, (d % 2) * T:(d % 2 + 1) * T], w2r[:, s, d * P:(d + 1) * P], hid0[:, f % 4, :],
                             f == 0 and d % 2 == 0, f == NF - 1, skip_group_check=True)
                ins.then_inc(down_done, 1)

            up(0)
            up(1)
            pe.wait_ge(res_done, 8)
            for f in range(NF):
                if f + 2 < NF:
                    up(f + 2)
                down(f)


            norm_mean(2, 4)
            pe.wait_ge(in_xm, 48)
            for a in range(2):
                for k in range(KD):
                    if a == 0:
                        pe.wait_ge(xn_done, 2 * KD + k + 1)
                    ins = mm(ps[0:8, 5, a * T:(a + 1) * T], wgt[:, k, 8 * a:8 * a + 8], xn[:, k, :], k == 0, k == KD - 1)
            ins.then_inc(gt_done, 1)
            pe.wait_ge(res_done, 16)
            for i in range(8):
                w, c0 = (wxm, 2 * i * P) if i < 4 else (wz, (2 * i - 8) * P)
                if i == 4:
                    pe.wait_ge(in_z, 16)
                if i >= 4:
                    pe.wait_ge(xm_out, i - 3)
                for u in range(2):
                    for k in range(KD):
                        ins = mm(ps[:, i % 4, u * T:(u + 1) * T], w[:, k, c0 + u * P:c0 + (u + 1) * P], xn[:, k, :], k == 0, k == KD - 1)
                ins.then_inc(p1, 1)
            pe.wait_ge(row_g, 1)
            for c in range(CH):
                ins = nc.tensor.transpose(ps[:, 5, 8 * c:8 * c + 8], row[:, 8, c * P:(c + 1) * P], cf[0:8, IDENT:IDENT + 8])
            ins.then_inc(gtr_done, 1)
            pe.wait_ge(in_qkv, 16)
            for i in range(4):
                b0 = 4 * (i % 2)
                pe.wait_ge(xc_done, 2 * i + 2)
                if i == 0:
                    pe.wait_ge(z_out, 4)
                if i == 1:
                    pe.wait_ge(gtok_out, 1)
                if i >= 2:
                    pe.wait_ge(qk_out, i - 1)
                    pe.wait_ge(kv_out, i - 1)
                for u in range(2):
                    h = 2 * i + u
                    for a in range(2):
                        mm(ps[:, b0 + a, u * T:(u + 1) * T], wqkv[:, a, h, :], xc1[:, h, :], True, True)
                    for c in range(CH):
                        o = slice(u * T + c * P, u * T + (c + 1) * P)
                        mm(ps[:, b0 + 2, o], xc1[:, h, c * P:(c + 1) * P], wqkv[:, 1, h, :], True, True)
                        ins = mm(ps[:, b0 + 3, o], xmp[:, h, 3 + c * P:3 + (c + 1) * P], wqkv[:, 2, h, :], True, True)
                ins.then_inc(qkv_done, 1)

            def spread(h):
                b0 = 4 * (h % 2)
                if h >= 2:
                    pe.wait_ge(enm_out, h - 1)
                    pe.wait_ge(qsc_done, h - 1)
                    pe.wait_ge(cn_out, h - 1)
                    pe.wait_ge(sT_done, h - 1)
                mm(ps[:, b0, :], sel[:, h, :], row[:, 2:4, :].rearrange("p n t -> p (n t)"), True, True)
                mm(ps[:, b0 + 1, 0:P], sel[:, h, :], row[:, 4, 0:P], True, True).then_inc(bc_done, 1)
                for c in range(CH):
                    ins = mm(ps[:, b0 + 2, c * P:(c + 1) * P], k1[:, h, c * P:(c + 1) * P], q1[:, h, c * P:(c + 1) * P], True, True)
                ins.then_inc(kq_done, 1)

            pe.wait_ge(rows_done, 2)
            pe.wait_ge(qk_out, 4)
            pe.wait_ge(kv_out, 4)
            spread(0)
            for h in range(8):
                if h < 7:
                    spread(h + 1)
                b0, s = 4 * (h % 2), h % 2
                pe.wait_ge(kw_done, h + 1)
                pe.wait_ge(qsc_done, h + 1)
                mm(ps[:, b0 + 1, T:T + P], kw[:, s, :], vt1[:, h, 0, :], True, True)
                mm(ps[:, b0 + 1, T + P:2 * T], kw[:, s, :], con(ONES), True, True).then_inc(cn_done, 1)
                pe.wait_ge(sT_done, h + 1)
                pe.wait_ge(cn_out, h + 1)
                if h >= 2:
                    pe.wait_ge(h_done, h - 1)
                for a in range(2):
                    o = a * T
                    mm(ps[:, b0 + 3, o:o + P], con(ONES) if a else vt1[:, h, 0, :], sT[:, s, 0:P], True, True)
                    mm(ps[:, b0 + 3, o + P:o + T], con(ONES) if a else vt1[:, h, 1, :], sT[:, s, P:T], True, False)
                    ins = mm(ps[:, b0 + 3, o + P:o + T], CN[:, s, a * P:(a + 1) * P], qsc[:, s, :], False, True)
                ins.then_inc(nd_done, 1)
            pe.wait_ge(h_done, 8)
            for i in range(4):
                pe.wait_ge(hsq_done, i + 1)
                mm(ps[:, i, :], con(MEAN_H), xc1[:, 2 * i:2 * i + 2, :].rearrange("p j t -> p (j t)"), True, True).then_inc(hm_done, 1)
            pe.wait_ge(hroot_done, 4)
            pe.wait_ge(in_wo1, 16)
            for i in range(4):
                pe.wait_ge(y1_done, 2 * i + 2)
                project_out(wo1, range(KD), range(2 * i, 2 * i + 2))

            norm_mean(3, 4)
            pe.wait_ge(in_rt, 16)
            for c in range(CH):
                for k in range(KD):
                    if c == 0:
                        pe.wait_ge(xn_done, 3 * KD + k + 1)
                    ins = mm(ps[:, 5, 8 * c:8 * c + 8], xn[:, k, c * P:(c + 1) * P], wrt[:, k, :], k == 0, k == KD - 1)
            ins.then_inc(lg_done, 1)
            for c in range(CH):
                for i in range(2):
                    for k in range(4):
                        ins = nc.tensor.transpose(ps[:, 2 * c + i, k * P:(k + 1) * P], xn[:, 4 * i + k, c * P:(c + 1) * P], con(IDENT))
                    ins.then_inc(tk_done, 1)
            pe.wait_ge(sel_done, 1)
            mm(ps[:, 5, 16:24], con(SU), rt[:, 12, :], True, True)
            mm(ps[:, 5, 24:32], con(ONES), rt[:, 12, :], True, False)
            mm(ps[:, 5, 24:32], con(SU), rt[:, 13, :], False, True)
            mm(ps[:, 5, 32:40], con(ONES), rt[:, 12, :], True, False)
            mm(ps[:, 5, 32:40], con(ONES), rt[:, 13, :], False, True).then_inc(pos_done, 1)

            def gather_matrices(n):
                for e in range(E):
                    pe.wait_ge(ohg_done, E * n + e + 1)
                    if e >= 2:
                        pe.wait_ge(sg_out, E * n + e - 1)
                    for c in range(CH):
                        ins = nc.tensor.transpose(ps[:, 6 + e % 2, c * P:(c + 1) * P], OHg[:, e % 2, c, :], con(IDENT))
                    ins.then_inc(sgt_done, 1)

            def gather(e, gx):
                pe.wait_ge(m_add, gx * 2)
                for k in range(KD):
                    for c in range(CH):
                        ins = mm(ps[:, 2 + k // 4, (k % 4) * SLOTS:(k % 4 + 1) * SLOTS], xtok[:, c, k * P:(k + 1) * P],
                                 OH[:, e, c, :], c == 0, c == 1)
                ins.then_inc(m_gather, 1)

            def scatter(e, ge, gx, r):
                if r == 0:
                    pe.wait_ge(m_yout, ge + 1)
                    pe.wait_ge(m_xg, gx + 1)
                else:
                    pe.wait_ge(m_add, gx * 2 + 1)
                for d in range(4):
                    ins = mm(ps[:, 2 + d // 2, (d % 2) * T:(d % 2 + 1) * T], ye[:, (4 * r + d) * P:(4 * r + d + 1) * P],
                             SG[:, e, :], True, True)
                ins.then_inc(m_sc, 1)

            def expert(e, ge, gx, b):
                def landed(s, f):
                    h, slot = divmod(f, RS)
                    if slot % 4 == 0:
                        pe.wait_ge(s[min(slot // 4, 2)], (ge * 2 + (h + 3)) * 16)

                def up(p):
                    pe.wait_ge(m_hid, ge * RS + p + 9)
                    for u in range(2):
                        f = 2 * p + u
                        landed(in_w1, f)
                        landed(in_w3, f)
                    for a, w in enumerate((w1r, w3r)):
                        for u in range(2):
                            s0 = (2 * p + u) % RS * P
                            o = a * T + u * SLOTS
                            for k in range(KD):
                                ins = mm(ps[:, 4 + p % 4, o:o + SLOTS], w[:, k, s0:s0 + P], xg[:, b, k, :], k == 0, k == KD - 1)
                    ins.then_inc(m_up, 1)

                def down(p):
                    pe.wait_ge(m_hid, ge * RS + p + 12)
                    for turn in range(3):
                        if turn < 2:
                            landed(in_w2, 2 * p + turn)
                        for g in range(4):
                            i, odd = divmod(g, 2)
                            u, t = (odd, 1) if turn == 2 else (turn, 2 * odd)
                            ins = mm(ps[32 * g:32 * g + 32, turn // 2, :], hid[:, p % 4, u, 32 * t:32 * t + 32],
                                     w2r[:, (2 * p + u) % RS, 512 * i:512 * (i + 1)], p == 0 and turn != 1, p == RS - 1 and turn != 0,
                                     skip_group_check=True)
                    ins.then_inc(m_down, 1)

                pe.wait_ge(m_xg, gx + 1)
                up(0)
                up(1)
                for p in range(RS):
                    if p + 2 < RS:
                        up(p + 2)
                    if p == 0:
                        pe.wait_ge(m_yout, ge + 1)
                    down(p)
                    if p in (1, 3):
                        scatter(e, ge, gx, p // 2)
                    if p == 6:
                        gather(e + 1, gx + 1)

            def experts(n):
                pe.wait_ge(sg_out, E * (n + 1))
                with pe.Fori(0, E // 2) as i:
                    for b in range(2):
                        expert(i * 2 + b, i * 2 + (b + E * n), i * 2 + (b + (E + 1) * n), b)
                for r in range(2):
                    scatter(E, E * (n + 1), (E + 1) * n + E, r)

            pe.wait_ge(tk_out, 4)
            gather_first = [(k, c) for k in range(KD) for c in range(CH)]
            pe.wait_ge(oh_done, 1)
            for k, c in gather_first:
                ins = mm(ps[:, 2 + k // 4, (k % 4) * SLOTS:(k % 4 + 1) * SLOTS], xtok[:, c, k * P:(k + 1) * P], OH[:, 0, c, :], c == 0, c == 1)
            ins.then_inc(m_gather, 1)
            gather_matrices(0)
            pe.wait_ge(moe_zero, 2)
            experts(0)
            pe.wait_ge(flag_done, 1)
            over = pe.value_load(flag[0:1, 0:1], min_val=0, max_val=1)
            with pe.If(over != 0):
                for n in range(1, PASSES):
                    pe.wait_ge(oh_done, n + 1)
                    pe.wait_ge(m_add, (2 * E + 2) * n)
                    for k, c in gather_first:
                        ins = mm(ps[:, 2 + k // 4, (k % 4) * SLOTS:(k % 4 + 1) * SLOTS], xtok[:, c, k * P:(k + 1) * P], OH[:, 0, c, :], c == 0, c == 1)
                    ins.then_inc(m_gather, 1)
                    gather_matrices(n)
                    experts(n)
            norm_mean(4, 4)

        @block.scalar
        def _(act):
            n = [0]

            def step(ins):
                n[0] += 1
                ins.then_inc(act_seq, 1)
                act.wait_ge(act_seq, n[0])

            A_ = nc.scalar.activation
            act.dma_start(vec[:, :], A["vecs"]).then_inc(in_con, 16)
            act.dma_start(lmf, A["lm"]).then_inc(in_late, 16)
            act.dma_start(gb[:, :], A["gb"]).then_inc(in_late, 16)

            def norm_squares(ready, each):
                for k in range(KD):
                    ready(k)
                    A_(xn[:, k, :], x[:, k, :], ACT.Square).then_inc(sq_done, 1)

            def norm_root(i, bank):
                A_(misc[:, 86:87], con(EPS, n=1), ACT.Sqrt)
                act.wait_ge(mean_done, i + 1)
                if i:
                    act.wait_ge(xn_done, KD * i)
                A_(rs[:, :], ps[:, bank, 0:T], ACT.Sqrt, bias=con(EPS, n=1)).then_inc(root_done, 1)

            act.wait_ge(in_x, 16)
            norm_squares(lambda k: None, None)
            act.wait_ge(in_con, 32)
            norm_root(0, 4)
            step(A_(SPM, vec[:, VECS["l0_lru_lambda"]:VECS["l0_lru_lambda"] + 4], ACT.Abs))
            A_(SPM, SPM, ACT.Exp, scale=-1.0).then_inc(lam_exp, 1)

            def shifted(i):
                act.wait_ge(proj, i + 1)
                act.wait_ge(omm_done, 1)
                for u in range(2):
                    m = MIXAT[PAIRS[i][2] + u]
                    A_(mix[:, m, :], ps[:, i % 4, u * T:(u + 1) * T], ACT.Copy, scale=OMM[:, m:m + 1]).then_inc(part, 1)

            shifted(0)
            act.wait_ge(mixed, 2)
            A_(mix[0:HD, 12, :], mix[0:HD, 12, :], ACT.Tanh).then_inc(lora_act, 1)
            A_(mix[:, 13, :], mix[:, 13, :], ACT.Sigmoid).then_inc(lora_act, 1)
            shifted(1)
            shifted(2)
            act.wait_ge(kk_ready, 1)
            A_(tmp[:, :, :], kk[:, :, :], ACT.Square).then_inc(kk_sq, 1)
            act.wait_ge(z_done, 1)
            act.wait_ge(proj, 5)
            for j in range(4):
                ins = A_(sg[:, j, :], ps[:, 6 + j // 2, (j % 2) * T:(j % 2 + 1) * T], ACT.Sigmoid, bias=col("l0_w0", j))
            ins.then_inc(sg_done, 1)
            shifted(3)
            shifted(4)
            act.wait_ge(am_done, 1)
            for j in range(4):
                ins = A_(a_[:, j, :], ps[:, 6 + j // 2, (j % 2) * T:(j % 2 + 1) * T], ACT.Sigmoid, bias=col("l0_a0", j))
            ins.then_inc(a_done, 1)
            act.wait_ge(kk_sum, 1)
            A_(tmp[:, :, :].rearrange("p j t -> p (j t)"), ps[:, 4:6, :].rearrange("p b n -> p (b n)"), ACT.Sqrt).then_inc(kk_root, 1)
            shifted(5)
            shifted(6)
            act.wait_ge(g_done, 1)
            A_(gate_rw[:, :, :].rearrange("p j t -> p (j t)"), ps[:, 4:6, :].rearrange("p b n -> p (b n)"), ACT.Copy).then_inc(g_out, 1)
            act.wait_ge(cum_done, 1)
            for j in range(4):
                for c in range(CH):
                    i = CH * j + c
                    A_(Ep[:, j, c, :], Gp[:, j, c, :], ACT.Exp, scale=-DECAY, bias=CPOS[:, i:i + 1])
                    ins = A_(Em[:, j, c, :], Gp[:, j, c, 1:P + 1], ACT.Exp, scale=DECAY, bias=CNEG[:, i:i + 1])
            ins.then_inc(e_done, 1)
            A_(DSC, DSC, ACT.Exp, scale=-DECAY).then_inc(e_done, 1)
            act.wait_ge(zeroed, 1)
            for i in (7, 8):
                act.wait_ge(proj, i + 1)
                for u in range(2):
                    A_(lxp[:, 2 * (i - 7) + u, 3:259], ps[:, i % 4, u * T:(u + 1) * T], ACT.Copy).then_inc(lgact, 1)
            for i in (9, 10):
                act.wait_ge(proj, i + 1)
                for u in range(2):
                    A_(gelu[:, 2 * (i - 9) + u, :], ps[:, i % 4, u * T:(u + 1) * T], ACT.Gelu_apprx_tanh).then_inc(lgact, 1)

            def tr_evac(dst, i):
                act.wait_ge(tr_done, i + 1)
                A_(dst[:, i % 2, :, :].rearrange("p j v -> p (j v)"), ps[:, 4 + i % 4, :], ACT.Copy).then_inc(tr_out, 1)

            tr_evac(Vt, 0)
            tr_evac(Vt, 1)
            for a, (dst, b) in enumerate(((lr, "l0_gate_a_b"), (li, "l0_gate_x_b"))):
                act.wait_ge(lgate, a + 1)
                for j in range(4):
                    ins = A_(dst[:, j, :], ps[:, 2 * a + j // 2, (j % 2) * T:(j % 2 + 1) * T], ACT.Sigmoid, bias=col(b, j))
                ins.then_inc(lgate_out, 1)
            for i in range(2, 6):
                tr_evac((Vt, Bt, Ktk)[i // 2], i)
            act.wait_ge(sp4_done, 1)
            act.wait_ge(lgate_out, 2)
            for j in range(4):
                ins = A_(lt[:, j, :], lr[:, j, :], ACT.Tanh, scale=SP4[:, j:j + 1])
            ins.then_inc(lth, 1)
            act.wait_ge(lth, 1)
            A_(lr[:, :, :], lt[:, :, :], ACT.Sqrt).then_inc(lroot, 1)

            for lv in range(1, LV):
                for q in range(4):
                    act.wait_ge(zmm, 4 * (lv - 1) + q + 1)
                    A_(Z[:, q].rearrange("p j t -> p (j t)"), ps[:, q, :], ACT.Copy).then_inc(zcp, 1)

            for c in range(CH):
                act.wait_ge(nv_done, c + 1)
                if c == 0:
                    act.wait_ge(xmm, 4 * (LV - 1))
                if c == 1:
                    pairs = ps[:, 1, :].rearrange("p (j u v) -> p j u v", j=4, u=2)
                    A_(RHS[:, c].rearrange("p (j u) v -> p j u v", u=2)[:, :, 0, :], pairs[:, :, 0, :], ACT.Copy)
                    odd = ps[:, 0, :].rearrange("p (j u v) -> p j u v", j=4, u=2)
                    A_(RHS[:, c].rearrange("p (j u) v -> p j u v", u=2)[:, :, 1, :], odd[:, :, 1, :], ACT.Copy).then_inc(nv_out, 1)
                else:
                    A_(RHS[:, c].rearrange("p h v -> p (h v)"), ps[:, c, :], ACT.Copy).then_inc(nv_out, 1)
                act.wait_ge(u_done, c + 1)
                A_(U[:, c].rearrange("p h v -> p (h v)"), ps[:, 2, :], ACT.Copy).then_inc(u_out, 1)
                act.wait_ge(y_done, c + 1)
                for par in range(2):
                    A_(y0[half(par), :, c, :], ps[half(par), 4 + 2 * par + c, :].rearrange("p (j t) -> p j t", j=4),
                       ACT.Copy).then_inc(y_out, 1)
            act.wait_ge(ln_c, 1)
            A_(y0f[:, :, :], y1f[:, :, :], ACT.Square).then_inc(ln_sq, 1)
            act.wait_ge(ln_mm, 2)
            A_(y0f[:, :, :].rearrange("p j t -> p (j t)"), ps[:, 4:6, :].rearrange("p b n -> p (b n)"), ACT.Sqrt,
               bias=con(EPS + 1, n=1)).then_inc(ln_root, 1)

            act.wait_ge(wo_done, 4)
            norm_squares(lambda k: act.wait_ge(res_done, k + 1), None)
            norm_root(1, 4)
            for f in range(NF):
                act.wait_ge(up_done, f + 1)
                if f >= 4:
                    act.wait_ge(hid_done, f - 3)
                A_(sil0[:, f % 4, :], ps[:, 4 + f % 4, 0:T], ACT.Silu).then_inc(silu_done, 1)

            norm_squares(lambda k: act.wait_ge(res_done, 8 + k + 1), None)
            norm_root(2, 4)
            act.wait_ge(gt_done, 1)
            act.wait_ge(in_late, 32)
            A_(row[:, 0, :], ps[0:8, 5, 0:T], ACT.Identity, bias=gb[:, 0:1])
            A_(row[:, 1, :], ps[0:8, 5, T:2 * T], ACT.Identity, bias=gb[:, 1:2])
            step(A_(row[:, 2, :], ps[0:8, 5, T:2 * T], ACT.Abs, bias=gb[:, 1:2]))
            A_(row[:, 2, :], row[:, 2, :], ACT.Exp, scale=-1.0).then_inc(rows_in, 1)
            for i in range(4):
                act.wait_ge(p1, i + 1)
                A_(xmp[:, 2 * i:2 * i + 2, 3:259], ps[:, i, :].rearrange("p (u t) -> p u t", u=2), ACT.Copy).then_inc(xm_out, 1)
            for j in range(8):
                act.wait_ge(conv1, j + 1)
                A_(xc1[:, j, :], xc1[:, j, :], ACT.Silu, bias=col("l1_conv_b", j)).then_inc(xc_done, 1)
            for i in range(4):
                act.wait_ge(p1, i + 5)
                A_(zs[:, 2 * i:2 * i + 2, :], ps[:, i, :].rearrange("p (u t) -> p u t", u=2), ACT.Sigmoid).then_inc(z_out, 1)
            act.wait_ge(gtr_done, 1)
            A_(gtok[:, :, :], ps[:, 5, 0:16].rearrange("p (c h) -> p c h", c=CH), ACT.Copy).then_inc(gtok_out, 1)
            act.wait_ge(row_m, 1)
            A_(row[:, 3, :], row[:, 3, :], ACT.Exp, scale=-1.0).then_inc(rows_done, 1)
            A_(row[:, 4, 0:P], row[:, 2, P:T], ACT.Exp, scale=-1.0, bias=row[:, 9, 0:1]).then_inc(rows_done, 1)
            for i in range(4):
                b0 = 4 * (i % 2)
                act.wait_ge(qkv_done, i + 1)
                A_(q1[:, 2 * i:2 * i + 2, :], ps[:, b0, :].rearrange("p (u t) -> p u t", u=2), ACT.Copy, scale=float(P) ** -0.5)
                A_(k1[:, 2 * i:2 * i + 2, :], ps[:, b0 + 1, :].rearrange("p (u t) -> p u t", u=2), ACT.Copy).then_inc(qk_out, 1)
            for h in range(8):
                b0, s = 4 * (h % 2), h % 2
                act.wait_ge(dlog_done, h + 1)
                if h >= 2:
                    act.wait_ge(sT_done, h - 1)
                A_(dmat[:, s, :], dlog[:, s, :], ACT.Exp, scale=-1.0).then_inc(exp_done, 1)
                A_(wts[:, h:h + 1], ps[:, b0, P - 1:P], ACT.Exp, scale=-1.0, bias=gtok[:, 0, h:h + 1]).then_inc(wts_done, 1)
                if h >= 2:
                    act.wait_ge(h_done, h - 1)
                A_(enm[:, s, :], ps[:, b0, T:2 * T], ACT.Copy).then_inc(enm_out, 1)
                act.wait_ge(cn_done, h + 1)
                A_(CN[:, s, :], ps[:, b0 + 1, T:2 * T], ACT.Copy).then_inc(cn_out, 1)
            for i in range(4):
                act.wait_ge(h_done, 2 * i + 2)
                A_(xc1[:, 2 * i:2 * i + 2, :], h1[:, 2 * i:2 * i + 2, :], ACT.Square).then_inc(hsq_done, 1)
            A_(misc[:, 86:87], con(EPS, n=1), ACT.Sqrt)
            act.wait_ge(h_done, 8)
            for i in range(4):
                act.wait_ge(hm_done, i + 1)
                A_(q1[:, 2 * i:2 * i + 2, :], ps[:, i, :].rearrange("p (u t) -> p u t", u=2), ACT.Sqrt, bias=con(EPS, n=1)).then_inc(hroot_done, 1)

            act.wait_ge(wo_done, 8)
            norm_squares(lambda k: act.wait_ge(res_done, 16 + k + 1), None)
            norm_root(3, 4)
            for u in range(4):
                act.wait_ge(tk_done, u + 1)
                A_(xtok[:, u // 2, (u % 2) * 512:(u % 2 + 1) * 512], ps[:, u, :], ACT.Copy).then_inc(tk_out, 1)
            act.wait_ge(rt_exp_in, 1)
            A_(rt[:, 6, 0:2], rt[:, 6, 0:2], ACT.Exp).then_inc(rt_exp, 1)

            def gather_matrices(n):
                for e in range(E):
                    act.wait_ge(sgt_done, E * n + e + 1)
                    A_(SG[:, e + 1, :], ps[:, 6 + e % 2, 0:T], ACT.Copy).then_inc(sg_out, 1)

            def gathered(b, gx):
                act.wait_ge(m_gather, gx + 1)
                A_(xg[:, b, :, :].rearrange("p (a k) s -> p a (k s)", a=2), ps[:, 2:4, 0:4 * SLOTS], ACT.Copy).then_inc(m_xg, 1)

            def expert(ge, gx, b):
                for p in range(RS):
                    act.wait_ge(m_up, ge * RS + p + 12)
                    act.wait_ge(m_hid, ge * RS + p + 11)
                    A_(sil[:, p % 2, :], ps[:, 4 + p % 4, 0:2 * SLOTS], ACT.Silu).then_inc(m_silu, 1)
                    if p == 8:
                        gathered(1 - b, gx + 1)
                act.wait_ge(m_down, ge * RS + 22)
                for i in range(2):
                    for b2 in range(2):
                        ins = A_(ye[64 * b2:64 * b2 + 64, 512 * i:512 * (i + 1)], ps[64 * i:64 * i + 64, b2, :], ACT.Copy)
                ins.then_inc(m_yout, 1)

            def experts(n):
                with act.Fori(0, E // 2) as i:
                    for b in range(2):
                        expert(i * 2 + (b + E * n), i * 2 + (b + (E + 1) * n), b)

            act.wait_ge(m_yout, 1)
            gathered(0, 0)
            gather_matrices(0)
            experts(0)
            act.wait_ge(flag_done, 1)
            over = act.value_load(flag[0:1, 0:1], min_val=0, max_val=1)
            with act.If(over != 0):
                for turn in range(1, PASSES):
                    gathered(0, (E + 1) * turn)
                    gather_matrices(turn)
                    experts(turn)
            act.wait_ge(x_final, 1)
            norm_squares(lambda k: None, None)
            norm_root(4, 4)

        @block.vector
        def _(dve):
            V = nc.vector
            n = {}

            def step(ins, s=dve_seq):
                n[s.name] = n.get(s.name, 0) + 1
                ins.then_inc(s, 1)
                dve.wait_ge(s, n[s.name])

            def log1p_exp(y, s, s2, acc, top, out_scale, out):
                step(V.tensor_scalar(s, y, 2.0, None, ALU.add))
                step(V.reciprocal(s, s))
                step(V.tensor_tensor(s, y, s, ALU.mult))
                step(V.tensor_tensor(s2, s, s, ALU.mult))
                step(V.tensor_scalar(acc, s2, 1.0 / 17, None, ALU.mult))
                for d in (15, 13, 11, 9, 7, 5, 3):
                    step(V.scalar_tensor_tensor(acc, acc, 1.0 / d, s2, ALU.add, ALU.mult))
                step(V.scalar_tensor_tensor(acc, acc, 1.0, s, ALU.add, ALU.mult))
                step(V.scalar_tensor_tensor(acc, acc, 2.0, top, ALU.mult, ALU.add))
                step(V.tensor_scalar(out, acc, out_scale, None, ALU.mult))

            def normed(i, name, dst):
                dve.wait_ge(root_done, i + 1)
                step(V.reciprocal(rs[:, :], rs[:, :]))
                for k in range(KD):
                    V.scalar_tensor_tensor(dst[:, k, :], x[:, k, :], col(name, k), rs[:, :], ALU.mult, ALU.mult).then_inc(xn_done, 1)

            dve.wait_ge(in_con, 32)
            mu0 = VECS["l0_shift_mu"]
            V.tensor_scalar(OMM, vec[:, mu0:mu0 + 14], -1.0, 1.0, ALU.mult, ALU.add).then_inc(omm_done, 1)
            V.tensor_scalar(OKA, vec[:, VECS["l0_k_a"]:VECS["l0_k_a"] + 4], -1.0, 1.0, ALU.mult, ALU.add)
            dve.wait_ge(in_x, 16)
            normed(0, "l0_norm_mix", xn)
            lam = vec[:, VECS["l0_lru_lambda"]:VECS["l0_lru_lambda"] + 4]
            step(V.tensor_scalar(misc[:, 8:12], lam, -1.0, 0.0, ALU.mult, ALU.max))
            dve.wait_ge(lam_exp, 1)
            log1p_exp(SPM, misc[:, 12:16], misc[:, 16:20], misc[:, 20:24], misc[:, 8:12], 4.0, SP4)
            V.tensor_scalar(misc[:, 24:28], SP4, 1.0, None, ALU.mult).then_inc(sp4_done, 1)

            def shift(i):
                dve.wait_ge(part, 2 * i + 2)
                for u in range(2):
                    m = MIXAT[PAIRS[i][2] + u]
                    V.scalar_tensor_tensor(mix[:, m, 1:T], ps[:, i % 4, u * T:(u + 1) * T - 1],
                                           vec[:, mu0 + m:mu0 + m + 1], mix[:, m, 1:T], ALU.mult, ALU.add).then_inc(mixed, 1)

            shift(0)
            shift(1)
            shift(2)
            dve.wait_ge(mixed, 6)
            for j in range(4):
                ins = V.tensor_scalar(kk[:, j, :], k_[:, j, :], col("l0_k_k", j), None, ALU.mult)
            ins.then_inc(kk_ready, 1)
            dve.wait_ge(proj, 5)
            step(V.memset(Gp[:, :, :, 0:1], 0.0))
            dve.wait_ge(sg_done, 1)
            for j in range(4):
                for c in range(CH):
                    ins = V.tensor_tensor_scan(Gp[:, j, c, 1:P + 1], con(ONES), sg[:, j, c * P:(c + 1) * P], 0.0, ALU.mult, ALU.add)
            step(ins)
            cpos = CPOS.rearrange("p (j c) -> p j c", j=4)
            cneg = CNEG.rearrange("p (j c) -> p j c", j=4)
            V.tensor_scalar(cpos, Gp[:, :, :, P // 2], DECAY, None, ALU.mult)
            V.tensor_scalar(cneg, Gp[:, :, :, P // 2], -DECAY, None, ALU.mult)
            step(V.tensor_tensor(DSC, Gp[:, :, 0, P], Gp[:, :, 0, P // 2], ALU.subtract))
            V.tensor_tensor(DSC, DSC, Gp[:, :, 1, P // 2], ALU.add).then_inc(cum_done, 1)
            shift(3)
            shift(4)
            dve.wait_ge(kk_root, 1)
            step(V.tensor_scalar(tmp[:, :, :], tmp[:, :, :], 1e-12, None, ALU.max))
            step(V.reciprocal(tmp[:, :, :], tmp[:, :, :]))
            step(V.tensor_tensor(kk[:, :, :], kk[:, :, :], tmp[:, :, :], ALU.mult))
            dve.wait_ge(a_done, 1)
            for j in range(4):
                ins = V.tensor_scalar(tmp[:, j, :], a_[:, j, :], col("l0_k_a", j), OKA[:, j:j + 1], ALU.mult, ALU.add)
            step(ins)
            step(V.tensor_tensor(k_[:, :, :], k_[:, :, :], tmp[:, :, :], ALU.mult))
            step(V.scalar_tensor_tensor(a_[:, :, :], kk[:, :, :], -1.0, a_[:, :, :], ALU.mult, ALU.mult))
            for j in range(4):
                V.scalar_tensor_tensor(rk[:, j, :], r_[:, j, :], col("l0_r_k", j), k_[:, j, :], ALU.mult, ALU.mult)
            dve.wait_ge(e_done, 2)
            dve.wait_ge(lm_ready, 1)
            sp4d = lambda t: t.rearrange("p j (c t) -> p j c t", c=CH)
            V.tensor_tensor(AR[:, :, :, 0, :].rearrange("p c j t -> p j c t"), sp4d(kk), Ep[:, :, :, 0:P], ALU.mult)
            V.tensor_tensor(AR[:, :, :, 1, :].rearrange("p c j t -> p j c t"), sp4d(r_), Ep[:, :, :, 1:P + 1], ALU.mult)
            V.tensor_tensor(Bm[:, :, :, :].rearrange("p c j t -> p j c t"), sp4d(a_), Em[:, :, :, :], ALU.mult)
            step(V.tensor_tensor(Kt[:, :, :, :].rearrange("p c j t -> p j c t"), sp4d(k_), Em[:, :, :, :], ALU.mult), ops_done)
            shift(5)
            shift(6)
            dve.wait_ge(lgact, 4)
            dve.wait_ge(proj, 9)
            for j in range(4):
                step(V.tensor_scalar(xc0[:, j, :], lxp[:, j, 3:259], col("l0_conv_w", 12 + j), col("l0_conv_b", j), ALU.mult, ALU.add))
                for w in (2, 1, 0):
                    ins = V.scalar_tensor_tensor(xc0[:, j, :], lxp[:, j, w:w + T], col("l0_conv_w", 4 * w + j), xc0[:, j, :], ALU.mult, ALU.add)
                    if (j, w) == (3, 0):
                        step(ins, conv0)
                    else:
                        step(ins)

            for q in range(4):
                dve.wait_ge(pair_done, 3 * q + 1)
                u0 = 5 * q

                def banks(u, n):
                    return [(u + i) % 8 for i in range(n)]

                for i, b in enumerate(banks(u0, 2)):
                    V.tensor_tensor(NR[:, q, 2 * i:2 * i + 2].rearrange("p j a t -> p j (a t)"), ps[:, b, :].rearrange("p (j n) -> p j n", j=2),
                                    cf[:, SU:SU + 2 * P].unsqueeze(1).broadcast_to([P, 2, 2 * P]), ALU.mult).then_inc(pair_out, 1)
                dve.wait_ge(pair_done, 3 * q + 2)
                dve.wait_ge(xt_init, q + 1)
                for i, b in enumerate(banks(u0 + 2, 2)):
                    src = ps[:, b, :].rearrange("p (j a t) -> p j a t", j=2, a=2)
                    V.tensor_tensor(RBt[:, q, 2 * i:2 * i + 2], src[:, :, 1, :], con(IU).unsqueeze(1).broadcast_to([P, 2, P]), ALU.mult)
                    V.copy_predicated(XT[:, q, 2 * i:2 * i + 2], lm[:, 0:P].unsqueeze(1).broadcast_to([P, 2, P]), src[:, :, 0, :]).then_inc(pair_out, 1)
                dve.wait_ge(pair_done, 3 * q + 3)
                b, = banks(u0 + 4, 1)
                src = ps[:, b, :].rearrange("p (j t) -> p j t", j=4)
                V.copy_predicated(X[:, q], lm[:, LV * P:(LV + 1) * P].unsqueeze(1).broadcast_to([P, 4, P]), src)
                V.tensor_tensor(M[:, q], src, con(SL).unsqueeze(1).broadcast_to([P, 4, P]), ALU.mult).then_inc(pair_out, 1)

            def lru(part):
                if part == 1:
                    dve.wait_ge(lroot, 1)
                    step(V.tensor_scalar(lt[:, :, :], lt[:, :, :], 1.0, None, ALU.add))
                    step(V.reciprocal(lt[:, :, :], lt[:, :, :]))
                if part == 2:
                    step(V.scalar_tensor_tensor(lr[:, :, :], lr[:, :, :], 2.0, lt[:, :, :], ALU.mult, ALU.mult))
                    V.memset(lr[:, :, 0:1], 1.0)
                    step(V.tensor_scalar(lt[:, :, :], lt[:, :, :], 2.0, -1.0, ALU.mult, ALU.add))
                if part == 3:
                    dve.wait_ge(lgate_out, 2)
                    step(V.tensor_tensor(li[:, :, :], li[:, :, :], xc0[:, :, :], ALU.mult))
                    step(V.tensor_tensor(li[:, :, :], li[:, :, :], lr[:, :, :], ALU.mult))
                if part == 4:
                    for j in range(4):
                        ins = V.tensor_tensor_scan(xc0[:, j, :], lt[:, j, :], li[:, j, :], 0.0, ALU.mult, ALU.add)
                    step(ins)
                if part == 5:
                    V.tensor_tensor(xn[:, 0:4, :], xc0[:, :, :], gelu[:, :, :], ALU.mult).then_inc(y_lru, 1)

            dve.wait_ge(lgact, 8)
            for lv in range(1, LV):
                for q in range(4):
                    dve.wait_ge(xmm, 4 * (lv - 1) + q + 1)
                    ins = V.copy_predicated(XT[:, q], lm[:, lv * P:(lv + 1) * P].unsqueeze(1).broadcast_to([P, 4, P]),
                                            ps[:, 4 + q, :].rearrange("p (j t) -> p j t", j=4))
                    if lv < LV - 1:
                        ins = V.copy_predicated(X[:, q], lm[:, (LV + lv) * P:(LV + lv + 1) * P].unsqueeze(1).broadcast_to([P, 4, P]),
                                                ps[:, q, :].rearrange("p (j t) -> p j t", j=4))
                    ins.then_inc(xcp, 1)
                lru(lv)

            dve.wait_ge(st_done, 1)
            V.tensor_tensor(ST[:, :, :], ps[:, 3, 0:4 * HD].rearrange("p (j v) -> p j v", j=4),
                            DSC.unsqueeze(2).broadcast_to([P, 4, HD]), ALU.mult).then_inc(st_out, 1)
            dve.wait_ge(y_out, 4)
            dve.wait_ge(ln_mm, 1)
            fl = lambda t: t[:, :, :].rearrange("p j t -> p (j t)")
            step(V.tensor_tensor(fl(y1f), fl(y0f), ps[:, 4:6, :].rearrange("p b n -> p (b n)"), ALU.subtract), ln_c)
            dve.wait_ge(bonus_mm, 1)
            step(V.tensor_tensor(fl(v_), fl(v_), ps[:, 6:8, :].rearrange("p b n -> p (b n)"), ALU.mult))
            dve.wait_ge(ln_root, 1)
            for i in range(2):
                j0 = slice(2 * i, 2 * i + 2)
                step(V.reciprocal(y0f[:, j0, :], y0f[:, j0, :]))
                step(V.tensor_tensor(y1f[:, j0, :], y1f[:, j0, :], y0f[:, j0, :], ALU.mult))
                for j in (2 * i, 2 * i + 1):
                    ins = V.tensor_scalar(y1f[:, j, :], y1f[:, j, :], col("l0_ln_x_w", j), col("l0_ln_x_b", j), ALU.mult, ALU.add)
                step(ins)
                step(V.tensor_tensor(y1f[:, j0, :], y1f[:, j0, :], v_[:, j0, :], ALU.add))
                V.tensor_tensor(xn[:, 4 + 2 * i:6 + 2 * i, :], y1f[:, j0, :], gate_rw[:, j0, :], ALU.mult).then_inc(y_rw, 1)

            def residual(k0, done, count):
                for d in range(4):
                    dve.wait_ge(done, count(d))
                    for u in range(2):
                        V.tensor_tensor(x[:, 2 * d + u, :], x[:, 2 * d + u, :], ps[:, d, u * T:(u + 1) * T], ALU.add).then_inc(res_done, 1)

            residual(0, wo_done, lambda d: d + 1)
            normed(1, "l0_norm_ffn", xn)
            for f in range(NF):
                dve.wait_ge(silu_done, f + 1)
                if f >= 4:
                    dve.wait_ge(down_done, f - 3)
                V.tensor_tensor(hid0[:, f % 4, :], sil0[:, f % 4, :], ps[:, 4 + f % 4, T:2 * T], ALU.mult).then_inc(hid_done, 1)
            residual(8, down_done, lambda d: NF)

            normed(2, "l1_norm_mix", xn)
            dve.wait_ge(rows_in, 1)
            step(V.tensor_scalar(row[:, 6, :], row[:, 1, :], -1.0, 0.0, ALU.mult, ALU.max))
            log1p_exp(row[:, 2, :], row[:, 3, :], row[:, 4, :], row[:, 5, :], row[:, 6, :], 1.0, row[:, 6, :])
            for c in range(CH):
                o = slice(c * P, (c + 1) * P)
                ins = V.tensor_tensor_scan(row[:, 7, o], cf[0:8, ONES:ONES + P], row[:, 6, o], 0.0, ALU.mult, ALU.subtract)
            step(ins)
            step(V.tensor_tensor(row[:, 8, :], row[:, 0, :], row[:, 7, :], ALU.subtract), row_g)
            step(V.tensor_tensor_scan(row[:, 2, 0:P], row[:, 8, 0:P], row[:, 8, 0:P], 0.0, ALU.max, ALU.max))
            step(V.tensor_tensor(row[:, 9, 0:1], row[:, 2, P - 1:P], row[:, 7, P - 1:P], ALU.add))
            step(V.tensor_tensor_scan(row[:, 2, P:T], row[:, 8, P:T], row[:, 8, P:T], row[:, 9, 0:1], ALU.max, ALU.max))
            step(V.tensor_tensor(row[:, 3, :], row[:, 2, :], row[:, 7, :], ALU.add), row_m)
            dve.wait_ge(zeroed, 2)
            for j in range(8):
                dve.wait_ge(xm_out, j // 2 + 1)
                step(V.tensor_scalar(xc1[:, j, :], xmp[:, j, 3:259], col("l1_conv_w", 24 + j), None, ALU.mult))
                for w in (2, 1, 0):
                    step(V.scalar_tensor_tensor(xc1[:, j, :], xmp[:, j, w:w + T], col("l1_conv_w", 8 * w + j), xc1[:, j, :], ALU.mult, ALU.add),
                         dve_seq if w else conv1)
            for i in range(4):
                b0 = 4 * (i % 2)
                dve.wait_ge(qkv_done, i + 1)
                V.tensor_copy(kt1[:, 2 * i:2 * i + 2].rearrange("p h c d -> p (h c d)"), ps[:, b0 + 2, :])
                V.tensor_copy(vt1[:, 2 * i:2 * i + 2].rearrange("p h c d -> p (h c d)"), ps[:, b0 + 3, :]).then_inc(kv_out, 1)

            def normalised(h):
                b0, s = 4 * (h % 2), h % 2
                dve.wait_ge(nd_done, h + 1)
                dve.wait_ge(enm_out, h + 1)
                step(V.tensor_tensor(den[:, s, :], enm[:, s, :], ps[:, b0 + 3, T:2 * T], ALU.max))
                step(V.scalar_tensor_tensor(den[:, s, :], ps[:, b0 + 3, T:2 * T], -1.0, den[:, s, :], ALU.mult, ALU.max))
                step(V.reciprocal(den[:, s, :], den[:, s, :]))
                V.tensor_tensor(h1[:, h, :], den[:, s, :], ps[:, b0 + 3, 0:T], ALU.mult).then_inc(h_done, 1)

            def exponent(h):
                b0, s = 4 * (h % 2), h % 2
                dve.wait_ge(bc_done, h + 1)
                if h >= 2:
                    dve.wait_ge(masked, h - 1)
                for c in range(CH):
                    ins = V.tensor_scalar(dlog[:, s, c * P:(c + 1) * P], ps[:, b0, c * P:(c + 1) * P], gtok[:, c, h:h + 1], 0.0, ALU.subtract, ALU.max)
                ins.then_inc(dlog_done, 1)
                V.tensor_tensor(qsc[:, s, :], q1[:, h, P:T], ps[:, b0 + 1, 0:P], ALU.mult).then_inc(qsc_done, 1)

            dve.wait_ge(kv_out, 4)
            dve.wait_ge(gtok_out, 1)
            exponent(0)
            for h in range(8):
                b0, s = 4 * (h % 2), h % 2
                dve.wait_ge(wts_done, h + 1)
                V.tensor_scalar(kw[:, s, :], kt1[:, h, 0, :], wts[:, h:h + 1], None, ALU.mult).then_inc(kw_done, 1)
                dve.wait_ge(masked, h + 1)
                dve.wait_ge(kq_done, h + 1)
                V.tensor_tensor(sT[:, s, :], dmat[:, s, :], ps[:, b0 + 2, 0:T], ALU.mult).then_inc(sT_done, 1)
                if h < 7:
                    exponent(h + 1)
                if h:
                    normalised(h - 1)
            normalised(7)
            dve.wait_ge(z_out, 4)
            for i in range(4):
                dve.wait_ge(hroot_done, i + 1)
                step(V.reciprocal(q1[:, 2 * i:2 * i + 2, :], q1[:, 2 * i:2 * i + 2, :]))
                for j in (2 * i, 2 * i + 1):
                    ins = V.scalar_tensor_tensor(h1[:, j, :], h1[:, j, :], col("l1_mh_norm_w", j), q1[:, j, :], ALU.mult, ALU.mult)
                step(ins)
                for j in (2 * i, 2 * i + 1):
                    V.tensor_tensor(h1[:, j, :], h1[:, j, :], zs[:, j, :], ALU.mult).then_inc(y1_done, 1)
            residual(16, wo_done, lambda d: 4 + d + 1)

            normed(3, "l1_norm_ffn", xn)
            dve.wait_ge(lg_done, 1)
            step(V.tensor_copy(rt[:, 0:2, :], ps[:, 5, 0:16].rearrange("p (c e) -> p c e", c=CH)))
            for c in range(CH):
                step(V.max(rt[:, 2 + c, :], rt[:, c, :]))
                step(V.max_index(idx[:, c, :], rt[:, 2 + c, :], rt[:, c, :]))
            V.tensor_copy(rt[:, 4:6, :], idx[:, :, :])
            step(V.tensor_tensor(rt[:, 6, 0:2], rt[:, 2:4, 1], rt[:, 2:4, 0], ALU.subtract), rt_exp_in)
            dve.wait_ge(rt_exp, 1)
            step(V.tensor_scalar(rt[:, 7, 0:2], rt[:, 6, 0:2], 1.0, None, ALU.add))
            step(V.reciprocal(rt[:, 7, 0:2], rt[:, 7, 0:2]))
            step(V.tensor_tensor(rt[:, 7, 2:4], rt[:, 7, 0:2], rt[:, 6, 0:2], ALU.mult))
            iota8 = cf[:, IOTA:IOTA + 8]
            for c in range(CH):
                V.tensor_scalar(rt[:, 8 + c, :], iota8, rt[:, 4 + c, 0:1], rt[:, 7, c:c + 1], ALU.is_equal, ALU.mult)
                V.tensor_scalar(rt[:, 10 + c, :], iota8, rt[:, 4 + c, 1:2], rt[:, 7, 2 + c:3 + c], ALU.is_equal, ALU.mult)
                step(V.tensor_scalar(rt[:, 12 + c, :], iota8, rt[:, 4 + c, 0:1], None, ALU.is_equal))
                step(V.scalar_tensor_tensor(rt[:, 12 + c, :], iota8, rt[:, 4 + c, 1:2], rt[:, 12 + c, :], ALU.is_equal, ALU.add))
            step(V.tensor_tensor(rt[:, 8:10, :], rt[:, 8:10, :], rt[:, 10:12, :], ALU.add), sel_done)
            dve.wait_ge(pos_done, 1)
            step(V.scalar_tensor_tensor(rt[:, 14:16, :], ps[:, 5, 16:32].rearrange("p (c e) -> p c e", c=CH), 1.0, rt[:, 12:14, :], ALU.add, ALU.mult))
            step(V.tensor_scalar(rt[:, 14:16, :], rt[:, 14:16, :], -1.0, None, ALU.add))
            step(V.reduce_max(rt[:, 6, 2:3], ps[:, 5, 32:40], AX.X))
            step(V.tensor_scalar(rt[:, 6, 3:4], rt[:, 6, 2:3], float(SLOTS), None, ALU.is_gt))
            V.tensor_copy(flag[0:1, 0:1], rt[0:1, 6, 3:4]).then_inc(flag_done, 1)

            def gather_matrices(n):
                for e in range(E):
                    for c in range(CH):
                        ins = V.tensor_scalar(OH[:, e, c, :], con(IOTA, n=SLOTS), rt[:, 14 + c, e:e + 1], None, ALU.is_equal)
                    if e == 0:
                        ins.then_inc(oh_done, 1)
                    if E * n + e >= 2:
                        dve.wait_ge(sgt_done, E * n + e - 1)
                    for c in range(CH):
                        ins = V.tensor_scalar(OHg[:, e % 2, c, :], con(ROWS), rt[:, 14 + c, e:e + 1], rt[:, 8 + c, e:e + 1], ALU.is_equal, ALU.mult)
                    ins.then_inc(ohg_done, 1)

            def add(gx, r):
                dve.wait_ge(m_sc, gx * 2 + (r + 1))
                V.tensor_tensor(x[:, 4 * r:4 * r + 4, :].rearrange("p d t -> p (d t)"), x[:, 4 * r:4 * r + 4, :].rearrange("p d t -> p (d t)"),
                                ps[:, 2:4, :].rearrange("p b n -> p (b n)"), ALU.add).then_inc(m_add, 1)

            def expert(ge, gx):
                for p in range(RS):
                    dve.wait_ge(m_silu, ge * RS + p + 1)
                    dve.wait_ge(m_down, ge * RS + p + 9)
                    V.tensor_tensor(hid[:, p % 4, :, :].rearrange("p f s -> p (f s)"), sil[:, p % 2, :], ps[:, 4 + p % 4, T:T + 2 * SLOTS], ALU.mult).then_inc(m_hid, 1)
                    if p in (3, 5):
                        add(gx, (p - 3) // 2)

            def experts(n):
                with dve.Fori(0, E // 2) as i:
                    for b in range(2):
                        expert(i * 2 + (b + E * n), i * 2 + (b + (E + 1) * n))
                for r in range(2):
                    add((E + 1) * n + E, r)

            gather_matrices(0)
            experts(0)
            dve.wait_ge(m_add, 2 * E + 2)
            over = dve.value_load(flag[0:1, 0:1], min_val=0, max_val=1)
            with dve.If(over != 0):
                for turn in range(1, PASSES):
                    step(V.tensor_scalar(rt[:, 14:16, :], rt[:, 14:16, :], -float(SLOTS), None, ALU.add), pos_shifted)
                    gather_matrices(turn)
                    experts(turn)
                    dve.wait_ge(m_add, (2 * E + 2) * (turn + 1))
            V.memset(misc[:, 90:91], 0.0).then_inc(x_final, 1)
            normed(4, "final_norm", xn)


def inputs_of(i):
    def a(name):
        return np.asarray(i[name])
    o = {}
    o["xT"] = np.ascontiguousarray(a("x")[0].T)
    vecs = np.zeros((P, NV), np.float32)
    for name, at in VECS.items():
        v = a(name).reshape(-1, P).T
        vecs[:, at:at + v.shape[1]] = v
    o["vecs"] = vecs
    small = np.zeros((P, 4, 4, P), np.float32)
    for g, name in enumerate(("l0_gate_a_w", "l0_gate_x_w")):
        w = a(name).reshape(4, 2, HD, HD)
        for u in range(2):
            small[HD * u:HD * u + HD, g, :, HD * u:HD * u + HD] = w[:, u].transpose(1, 0, 2)
    small[0:HD, 2] = a("l0_w_up").reshape(HD, 4, P)
    small[HD:, 2] = a("l0_a_up").reshape(HD, 4, P)
    small[:, 3] = a("l0_g_up").reshape(P, 4, P)
    o["small0"] = small.reshape(P, 2048)
    o["wqkv"] = np.ascontiguousarray(np.stack([a("l1_wq"), a("l1_wk"), a("l1_wv")]).transpose(2, 0, 1, 3)).reshape(P, 3 * D)
    o["wgt"] = np.ascontiguousarray(a("l1_w_in")[:, 2 * D:].reshape(KD, P, 16).transpose(1, 0, 2)).reshape(P, KD * 16)
    o["wrt"] = np.ascontiguousarray(a("l1_router").reshape(KD, P, E).transpose(1, 0, 2)).reshape(P, KD * E)
    o["gb"] = np.ascontiguousarray(np.stack([a("l1_ig_b"), a("l1_fg_b")], 1))
    for name in ("l0_w_in", "l0_w_out", "l0_ffn_w1", "l0_ffn_w3", "l0_ffn_w2", "l1_w_in", "l1_w_out",
                 "l1_moe_w1", "l1_moe_w3", "l1_moe_w2"):
        o[name] = np.ascontiguousarray(a(name))
    o["cf"], o["lm"], o["sel"] = constants()
    return o


def kernel(**inputs):
    import concourse.bacc as bacc
    from concourse.bass_utils import run_bass_kernel_spmd

    nc = bacc.Bacc("TRN2", target_bir_lowering=False, num_devices=1)
    arrays = {f"in_{k}": v for k, v in inputs_of(inputs).items()}
    A = {k[3:]: nc.dram_tensor(k, v.shape, mybir.dt.from_np(v.dtype), kind="ExternalInput").ap() for k, v in arrays.items()}
    out = nc.dram_tensor("out_T", (D, T), F32, kind="ExternalOutput").ap()
    hybrid_rglru_rwkv7_mlstm_moe(nc, A, out)
    r = run_bass_kernel_spmd(nc, [arrays], core_ids=[0])
    return np.ascontiguousarray(r.results[0]["out_T"].T).reshape(1, T, D)
```
